# Optimizing a Trainium2 kernel written in Bass

```python
import jax, jax.numpy as jnp
from jax import lax
import numpy as np

"""One inference step (1 layer) of a hybrid decoder with parallel head groups.

Layer: x + W_o [ MLA(h) ; MultiScalePool(h) ] with h = RMSNorm(x), then x + PEER(RMSNorm(x)).
Both mixers read one combined input projection of h; their outputs are concatenated
and mapped by one output projection.

Inputs:
  x_prompt        (BATCH, SEQ, D_MODEL)           positions 0..SEQ-1
  x_sample        (DEC_BATCH, DEC_SEQ, D_MODEL)   positions PAST_LEN..PAST_LEN+DEC_SEQ-1
  cache_kv_latent (N_PHYS, PAGE_SIZE, KV_LORA)    paged, normalised MLA latent rows
  cache_k_rope    (N_PHYS, PAGE_SIZE, QK_ROPE_DIM) paged, rotated decoupled rotary key rows
  state_pool      (DEC_BATCH, POOL_STATE, POOL_WIDTH) last 15 pooling-input rows
  page_table      (DEC_BATCH, PAST_LEN // PAGE_SIZE) int32 logical -> physical page
  followed by the weights.
Outputs (tuple):
  y_prompt        (BATCH, SEQ, D_MODEL)
  y_sample        (DEC_BATCH, DEC_SEQ, D_MODEL)
  kv_prompt       (BATCH, SEQ, KV_LORA)        new latent rows of the prompt group
  krope_prompt    (BATCH, SEQ, QK_ROPE_DIM)    new rotary key rows of the prompt group
  pool_prompt     (BATCH, POOL_STATE, POOL_WIDTH)
  kv_sample       (DEC_BATCH, DEC_SEQ, KV_LORA)
  krope_sample    (DEC_BATCH, DEC_SEQ, QK_ROPE_DIM)
  pool_sample     (DEC_BATCH, POOL_STATE, POOL_WIDTH)
"""

D_MODEL = 1024
BATCH = 1
SEQ = 1024
DEPTH = 1
DEC_BATCH = 8
DEC_SEQ = 4
PAST_LEN = 2048
PAGE_SIZE = 128

MLA_HEADS = 8
QK_NOPE_DIM = 64
QK_ROPE_DIM = 32
QK_HEAD_DIM = QK_NOPE_DIM + QK_ROPE_DIM
V_HEAD_DIM = 64
Q_LORA = 384
KV_LORA = 256
MLA_WIDTH = MLA_HEADS * V_HEAD_DIM
ROPE_THETA = 10000.0
SM_SCALE = QK_HEAD_DIM ** -0.5
Q_BLOCK = 128

POOL_WINDOWS = (2, 4, 8, 16)
POOL_GROUPS = len(POOL_WINDOWS)
POOL_WIDTH = D_MODEL // 2
POOL_GROUP_DIM = POOL_WIDTH // POOL_GROUPS
POOL_STATE = max(POOL_WINDOWS) - 1

MIX_WIDTH = MLA_WIDTH + POOL_WIDTH
IN_WIDTH = Q_LORA + KV_LORA + QK_ROPE_DIM + POOL_WIDTH

PEER_HEADS = 8
N_KEYS = 128
N_EXPERTS = N_KEYS * N_KEYS
PEER_TOPK = 16
PEER_KEY_DIM = 256
PEER_HALF = PEER_KEY_DIM // 2
PEER_BLOCK = 128

EPS = 1e-6

kernel_name = "hybrid_mla_pool_peer_step"

def rms_norm(x, g):
    xf = x.astype(jnp.float32)
    y = xf * lax.rsqrt(jnp.mean(xf * xf, axis=-1, keepdims=True) + EPS)
    return (y * g.astype(jnp.float32)).astype(x.dtype)

def rope_angles(pos):
    half = QK_ROPE_DIM // 2
    inv_freq = ROPE_THETA ** (-jnp.arange(half, dtype=jnp.float32) / half)
    ang = pos.astype(jnp.float32)[:, None] * inv_freq[None, :]
    return jnp.cos(ang), jnp.sin(ang)

def apply_rope(x, cos, sin):
    xf = x.astype(jnp.float32)
    x1, x2 = jnp.split(xf, 2, axis=-1)
    return jnp.concatenate([x1 * cos - x2 * sin, x2 * cos + x1 * sin], axis=-1).astype(x.dtype)

def mixer_front(x, pos, g_attn, w_in, g_q_lat, w_q_up, g_kv_lat, g_q_nope, g_q_rope):
    b, s, _ = x.shape
    h = rms_norm(x, g_attn)
    z = h @ w_in
    o1, o2, o3 = Q_LORA, Q_LORA + KV_LORA, Q_LORA + KV_LORA + QK_ROPE_DIM
    q_lat, c_raw, k_pe, p_in = z[..., :o1], z[..., o1:o2], z[..., o2:o3], z[..., o3:]
    c = rms_norm(c_raw, g_kv_lat)
    cos, sin = rope_angles(pos)
    k_pe_rot = apply_rope(k_pe, cos, sin)
    q = (rms_norm(q_lat, g_q_lat) @ w_q_up).reshape(b, s, MLA_HEADS, QK_HEAD_DIM)
    q = rms_norm(q, jnp.concatenate([g_q_nope, g_q_rope, g_q_rope]))
    q = jnp.concatenate([q[..., :QK_NOPE_DIM],
                         apply_rope(q[..., QK_NOPE_DIM:], cos[:, None, :], sin[:, None, :])], axis=-1)
    return q, c, k_pe_rot, p_in

def mla_keys(c, k_pe_rot, w_uk, g_k_nope, g_k_rope):
    k_nope = jnp.einsum('blc,chn->blhn', c, w_uk)
    k_pe = jnp.broadcast_to(k_pe_rot[:, :, None, :], k_nope.shape[:3] + (QK_ROPE_DIM,))
    return rms_norm(jnp.concatenate([k_nope, k_pe], axis=-1),
                    jnp.concatenate([g_k_nope, g_k_rope, g_k_rope]))

def attn_probs(q, k, mask):
    s = jnp.einsum('bqhd,blhd->bhql', q, k).astype(jnp.float32) * SM_SCALE
    s = jnp.where(mask, s, -jnp.inf)
    return jax.nn.softmax(s, axis=-1)

def mla_prompt(q, c, k_pe_rot, w_uk, w_uv, g_k_nope, g_k_rope):
    b, s = q.shape[:2]
    k = mla_keys(c, k_pe_rot, w_uk, g_k_nope, g_k_rope)
    v = jnp.einsum('blc,chv->blhv', c, w_uv)
    nq = s // Q_BLOCK
    q_blocks = q.reshape(b, nq, Q_BLOCK, MLA_HEADS, QK_HEAD_DIM).transpose(1, 0, 2, 3, 4)
    kpos = jnp.arange(s)

    def block(args):
        qb, i = args
        qpos = i * Q_BLOCK + jnp.arange(Q_BLOCK)
        p = attn_probs(qb, k, kpos[None, :] <= qpos[:, None])
        return jnp.einsum('bhql,blhv->bqhv', p.astype(v.dtype), v)

    o = lax.map(block, (q_blocks, jnp.arange(nq)))
    return o.transpose(1, 0, 2, 3, 4).reshape(b, s, MLA_WIDTH)

def mla_sample(q, c_new, kpe_new, cache_kv_latent, cache_k_rope, page_table,
               w_uk, w_uv, g_k_nope, g_k_rope):
    b, s = q.shape[:2]

    def one_seq(args):
        pages, qb, cb, rb = args
        c_past = cache_kv_latent[pages].reshape(-1, KV_LORA)
        r_past = cache_k_rope[pages].reshape(-1, QK_ROPE_DIM)
        past = c_past.shape[0]
        c_all = jnp.concatenate([c_past, cb.astype(c_past.dtype)], axis=0)[None]
        r_all = jnp.concatenate([r_past, rb.astype(r_past.dtype)], axis=0)[None]
        k = mla_keys(c_all, r_all, w_uk, g_k_nope, g_k_rope)
        mask = jnp.arange(past + s)[None, :] <= (past + jnp.arange(s))[:, None]
        p = attn_probs(qb[None], k, mask)
        o_lat = jnp.einsum('bhql,blc->bqhc', p.astype(c_all.dtype), c_all)
        return jnp.einsum('bqhc,chv->bqhv', o_lat, w_uv)[0]

    o = lax.map(one_seq, (page_table, q, c_new, kpe_new))
    return o.reshape(b, s, MLA_WIDTH)

def pool_mix(p_in, prev, start_pos, w_pool, pool_scale):
    b, s, _ = p_in.shape
    ext = jnp.concatenate([prev.astype(p_in.dtype), p_in], axis=1)
    csum = jnp.pad(jnp.cumsum(ext.astype(jnp.float32), axis=1), ((0, 0), (1, 0), (0, 0)))
    pos = start_pos + jnp.arange(s)
    end = csum[:, POOL_STATE + 1:]
    pooled = []
    for gi, w in enumerate(POOL_WINDOWS):
        lo, hi = gi * POOL_GROUP_DIM, (gi + 1) * POOL_GROUP_DIM
        start = csum[:, POOL_STATE + 1 - w: POOL_STATE + 1 - w + s, lo:hi]
        cnt = jnp.minimum(w, pos + 1).astype(jnp.float32)[None, :, None]
        pooled.append((end[..., lo:hi] - start) / cnt)
    pooled = jnp.concatenate(pooled, axis=-1) - p_in.astype(jnp.float32)
    y = jnp.einsum('bsgi,gio->bsgo',
                   pooled.reshape(b, s, POOL_GROUPS, POOL_GROUP_DIM).astype(p_in.dtype), w_pool)
    return y.reshape(b, s, POOL_WIDTH) * pool_scale, ext[:, -POOL_STATE:]

def peer_block(hb, w_pq, peer_keys, peer_u, peer_v):
    t = hb.shape[0]
    q = (hb @ w_pq).reshape(t, PEER_HEADS, 2, PEER_HALF)
    s = jnp.einsum('thpk,hpnk->thpn', q, peer_keys).astype(jnp.float32)
    sv, si = lax.top_k(s, PEER_TOPK)
    cand = sv[:, :, 0, :, None] + sv[:, :, 1, None, :]
    cidx = si[:, :, 0, :, None] * N_KEYS + si[:, :, 1, None, :]
    fv, fi = lax.top_k(cand.reshape(t, PEER_HEADS, PEER_TOPK * PEER_TOPK), PEER_TOPK)
    e = jnp.take_along_axis(cidx.reshape(t, PEER_HEADS, PEER_TOPK * PEER_TOPK), fi, axis=-1)
    g = jax.nn.softmax(fv, axis=-1)
    a = jax.nn.gelu(jnp.einsum('thkd,td->thk', peer_u[e], hb).astype(jnp.float32), approximate=False)
    return jnp.einsum('thk,thkd->td', (g * a).astype(hb.dtype), peer_v[e])

def peer(h, w_pq, peer_keys, peer_u, peer_v):
    b, s, d = h.shape
    n = b * s
    nb = -(-n // PEER_BLOCK)
    t = jnp.pad(h.reshape(n, d), ((0, nb * PEER_BLOCK - n), (0, 0)))
    out = lax.map(lambda tb: peer_block(tb, w_pq, peer_keys, peer_u, peer_v),
                  t.reshape(nb, PEER_BLOCK, d))
    return out.reshape(nb * PEER_BLOCK, d)[:n].reshape(b, s, d)

def setup_inputs(seed: int = 0) -> dict:
    key = jax.random.key(seed)
    ks = jax.random.split(key, 32)
    f32 = jnp.float32
    n_pages = PAST_LEN // PAGE_SIZE
    used = DEC_BATCH * n_pages
    n_phys = used + max(used // 4, 1)

    def nrm(k, shape, scale):
        return jax.random.normal(k, shape, f32) * scale

    def gain(k, n):
        return 1.0 + 0.05 * jax.random.normal(k, (n,), f32)

    page_table = jax.random.permutation(ks[5], n_phys)[:used].reshape(DEC_BATCH, n_pages).astype(jnp.int32)
    return {
        'x_prompt': nrm(ks[0], (BATCH, SEQ, D_MODEL), 1.0),
        'x_sample': nrm(ks[1], (DEC_BATCH, DEC_SEQ, D_MODEL), 1.0),
        'cache_kv_latent': nrm(ks[2], (n_phys, PAGE_SIZE, KV_LORA), 1.0),
        'cache_k_rope': nrm(ks[3], (n_phys, PAGE_SIZE, QK_ROPE_DIM), 1.0),
        'state_pool': nrm(ks[4], (DEC_BATCH, POOL_STATE, POOL_WIDTH), 1.0),
        'page_table': page_table,
        'g_attn': gain(ks[6], D_MODEL),
        'w_in': nrm(ks[7], (D_MODEL, IN_WIDTH), D_MODEL ** -0.5),
        'g_q_lat': gain(ks[8], Q_LORA),
        'w_q_up': nrm(ks[9], (Q_LORA, MLA_HEADS * QK_HEAD_DIM), Q_LORA ** -0.5),
        'g_kv_lat': gain(ks[10], KV_LORA),
        'g_q_nope': gain(ks[11], QK_NOPE_DIM),
        'g_q_rope': gain(ks[12], QK_ROPE_DIM // 2),
        'g_k_nope': gain(ks[13], QK_NOPE_DIM),
        'g_k_rope': gain(ks[14], QK_ROPE_DIM // 2),
        'w_uk': nrm(ks[15], (KV_LORA, MLA_HEADS, QK_NOPE_DIM), KV_LORA ** -0.5),
        'w_uv': nrm(ks[16], (KV_LORA, MLA_HEADS, V_HEAD_DIM), KV_LORA ** -0.5),
        'w_pool': nrm(ks[17], (POOL_GROUPS, POOL_GROUP_DIM, POOL_GROUP_DIM), POOL_GROUP_DIM ** -0.5),
        'pool_scale': gain(ks[18], POOL_WIDTH),
        'w_o': nrm(ks[19], (MIX_WIDTH, D_MODEL), MIX_WIDTH ** -0.5),
        'g_ffn': gain(ks[20], D_MODEL),
        'w_pq': nrm(ks[21], (D_MODEL, PEER_HEADS * PEER_KEY_DIM), D_MODEL ** -0.5),
        'peer_keys': nrm(ks[22], (PEER_HEADS, 2, N_KEYS, PEER_HALF), PEER_HALF ** -0.5),
        'peer_u': nrm(ks[23], (N_EXPERTS, D_MODEL), D_MODEL ** -0.5),
        'peer_v': nrm(ks[24], (N_EXPERTS, D_MODEL), 0.5),
    }

def reference(x_prompt, x_sample, cache_kv_latent, cache_k_rope, state_pool, page_table,
              g_attn, w_in, g_q_lat, w_q_up, g_kv_lat, g_q_nope, g_q_rope, g_k_nope, g_k_rope,
              w_uk, w_uv, w_pool, pool_scale, w_o, g_ffn, w_pq, peer_keys, peer_u, peer_v):
    yp, ys = x_prompt, x_sample
    past_len = page_table.shape[1] * cache_kv_latent.shape[1]
    for _ in range(DEPTH):
        pos_p = jnp.arange(yp.shape[1])
        q, kv_prompt, krope_prompt, p_in = mixer_front(yp, pos_p, g_attn, w_in, g_q_lat, w_q_up,
                                                       g_kv_lat, g_q_nope, g_q_rope)
        a = mla_prompt(q, kv_prompt, krope_prompt, w_uk, w_uv, g_k_nope, g_k_rope)
        zero_prev = jnp.zeros((yp.shape[0], POOL_STATE, POOL_WIDTH), p_in.dtype)
        pool_out, pool_prompt = pool_mix(p_in, zero_prev, 0, w_pool, pool_scale)
        yp = yp + jnp.concatenate([a, pool_out], axis=-1) @ w_o
        yp = yp + peer(rms_norm(yp, g_ffn), w_pq, peer_keys, peer_u, peer_v)

        pos_s = past_len + jnp.arange(ys.shape[1])
        q, kv_sample, krope_sample, p_in = mixer_front(ys, pos_s, g_attn, w_in, g_q_lat, w_q_up,
                                                       g_kv_lat, g_q_nope, g_q_rope)
        a = mla_sample(q, kv_sample, krope_sample, cache_kv_latent, cache_k_rope, page_table,
                       w_uk, w_uv, g_k_nope, g_k_rope)
        pool_out, pool_sample = pool_mix(p_in, state_pool, past_len, w_pool, pool_scale)
        ys = ys + jnp.concatenate([a, pool_out], axis=-1) @ w_o
        ys = ys + peer(rms_norm(ys, g_ffn), w_pq, peer_keys, peer_u, peer_v)
    return (yp, ys, kv_prompt, krope_prompt, pool_prompt, kv_sample, krope_sample, pool_sample)


_drawn_inputs = setup_inputs


def setup_inputs(seed=0):
    import zlib

    import numpy as np

    out = dict(_drawn_inputs(seed))
    spreads = {}
    factors = {'g_q_lat': 4.287,
     'g_q_nope': 3.82,
     'g_q_rope': 6.869,
     'g_k_nope': 4.545,
     'g_k_rope': 5.041}
    for name, (base, spread) in spreads.items():
        noise = np.random.default_rng([zlib.crc32(name.encode()), seed]).standard_normal(out[name].shape)
        drawn = base * np.exp(spread * noise) if base else spread * noise
        out[name] = __import__('jax').numpy.asarray(drawn.astype(out[name].dtype))
    for name, factor in factors.items():
        out[name] = (out[name] * factor).astype(out[name].dtype)
    return out
```

```python
from contextlib import ExitStack

import numpy as np

import concourse.bass as bass
from concourse import mybir

F32 = mybir.dt.float32
F32R = mybir.dt.float32r
U32 = mybir.dt.uint32
I32 = mybir.dt.int32
ALU = mybir.AluOpType
ACT = mybir.ActivationFunctionType
AX = mybir.AxisListType.X

P = 128
D = 1024
KD = D // P
SEQ = 1024
DEC_B, DEC_S = 8, 4
NS = DEC_B * DEC_S
NT = SEQ + NS
TILES = SEQ // P + 1
PT_TILES = SEQ // P
NPAD = TILES * P
PAST = 2048
PAGES = PAST // P
H = 8
NOPE, ROPE, VD = 64, 32, 64
HD = NOPE + ROPE
HALF = ROPE // 2
QL, KVL = 384, 256
QT, CT = QL // P, KVL // P
PW = 512
G4 = 4
WINDOWS = (2, 4, 8, 16)
PSTATE = 15
IN_W = QL + KVL + ROPE + PW
EPS = 1e-6
SM = HD ** -0.5
NK = 128
HP = 16
TOPK = 16
TB = NT // 3
GT = 88
GB = NT // GT
NEG = -3.0e38


def with_sems(nc, ctx, names):
    sems = {n: nc.alloc_semaphore(n) for n in names.split()}

    def release():
        nc.clear_and_free_semaphores(list(sems.values()))
        nc.all_engine_barrier()
    ctx.callback(release)
    return sems


def after(eng, sem, value):
    if isinstance(value, int) and value <= 0:
        return
    eng.wait_ge(sem, value)


def mixer_front(nc, a, qkT, vall):
    with ExitStack() as ctx:
        def sb(name, shape, dt=F32):
            return ctx.enter_context(nc.sbuf_tensor(name, shape, dt))

        w_in = sb("f_w_in", [P, KD, IN_W])
        w_q = sb("f_w_q", [P, QT, H * HD])
        w_uk = sb("f_w_uk", [P, CT, H * NOPE])
        w_uv = sb("f_w_uv", [P, CT, H * VD])
        g_attn = sb("f_g_attn", [P, KD])
        g_ql = sb("f_g_ql", [P, QT])
        g_kv = sb("f_g_kv", [P, KVL])
        g_qk = sb("f_g_qk", [P, 2, HD])
        rope_c = sb("f_rope_c", [P, TILES, ROPE])
        rope_s = sb("f_rope_s", [P, TILES, ROPE])
        ident = sb("f_ident", [P, P])
        eps = sb("f_eps", [P, 1])
        x_t = sb("f_x", [P, D])
        xT = sb("f_xT", [P, KD, P])
        junk = sb("f_junk", [P, 2 * H * HD])
        zq = sb("f_zq", [P, QL])
        zck = sb("f_zck", [P, KVL + ROPE])
        pin = sb("f_pin", [P, PW])
        c_t = sb("f_c", [P, KVL])
        kr = sb("f_kr", [P, ROPE])
        r_a = sb("f_ra", [P, H, ROPE])
        r_b = sb("f_rb", [P, H, ROPE])
        qlT = sb("f_qlT", [P, QT, P])
        cT = sb("f_cT", [P, CT, P])
        qk = sb("f_qk", [P, 2 * H, HD])
        ss = sb("f_ss", [P, 1])
        rstd = sb("f_rstd", [P, 1])
        ss2 = sb("f_ss2", [P, 2])
        rstd2 = sb("f_rstd2", [P, 2])
        ssh = sb("f_ssh", [P, 2 * H])
        rstdh = sb("f_rstdh", [P, 2 * H])
        banks = [ctx.enter_context(nc.psum_tensor(f"f_b{i}", [P, 512], F32)) for i in range(8)]

        s = with_sems(nc, ctx, """f_wts f_x_in f_consts f_w_scaled f_z f_sqx f_std f_rstd f_zq f_zck f_pin
            f_ms f_std2 f_rstd2 f_qlt f_qlT f_q f_qev f_c f_ct f_cT f_kv f_kev f_vev f_ra f_rb f_kr f_kpe
            f_sqh f_ssh f_stdh f_rstdh f_n1 f_n2 f_qra f_qrb f_rot f_tr0 f_tr1 f_ev0 f_ev1 f_out""")
        block = ctx.enter_context(nc.Block())

        @block.sync
        def _(sp):
            for dst, src in ((w_in, a["w_in"]), (w_q, a["w_q_up"]), (w_uk, a["w_uk"]), (w_uv, a["w_uv"]),
                             (g_attn, a["g_attn"]), (g_ql, a["g_q_lat"]), (ident, a["ident"]),
                             (rope_c, a["rope_c"]), (rope_s, a["rope_s"]),
                             (g_kv, a["g_kv_lat"].to_broadcast((P, KVL)))):
                sp.dma_start(dst[:], src).then_inc(s["f_wts"], 16)
            for i, n in enumerate(("q", "k")):
                sp.dma_start(g_qk[:, i, 0:NOPE], a[f"g_{n}_nope"].to_broadcast((P, NOPE))).then_inc(s["f_wts"], 16)
                for r in range(2):
                    sp.dma_start(g_qk[:, i, NOPE + r * HALF:NOPE + (r + 1) * HALF],
                                 a[f"g_{n}_rope"].to_broadcast((P, HALF))).then_inc(s["f_wts"], 16)

            def load(t):
                after(sp, s["f_z"], t)
                after(sp, s["f_sqx"], t)
                sp.dma_start(x_t[:], a["x"][bass.ds(t * P, P), :]).then_inc(s["f_x_in"], 16)
                sp.dma_start(xT[:], a["xT"][:, :, bass.ds(t * P, P)]).then_inc(s["f_x_in"], 16)
            load(0)

            def store(t):
                sp.wait_ge(s["f_pin"], t + 1)
                sp.dma_start(a["pin_d"][bass.ds(t * P, P), :], pin[:]).then_inc(s["f_out"], 16)
                sp.wait_ge(s["f_c"], t + 1)
                sp.dma_start(a["kv_all"][bass.ds(t * P, P), :], c_t[:]).then_inc(s["f_out"], 16)
                sp.wait_ge(s["f_kr"], t + 1)
                sp.dma_start(a["kr_all"][bass.ds(t * P, P), :], kr[:]).then_inc(s["f_out"], 16)
            with sp.Fori(0, TILES - 1) as t:
                load(t + 1)
                store(t)
            store(TILES - 1)
            sp.wait_ge(s["f_out"], 48 * TILES)

        @block.tensor
        def _(pe):
            pe.wait_ge(s["f_w_scaled"], 2)
            with pe.Fori(0, TILES) as t:
                pe.wait_ge(s["f_x_in"], 32 * t + 32)
                pe.wait_ge(s["f_ev1"], t)
                pe.wait_ge(s["f_kev"], t)
                pe.wait_ge(s["f_vev"], t)
                for b, lo, hi in ((0, 0, QL), (1, QL, QL + KVL + ROPE), (2, QL + KVL + ROPE, IN_W)):
                    for k in range(KD):
                        mm = pe.matmul(banks[b][:, 0:hi - lo], xT[:, k, :], w_in[:, k, lo:hi],
                                       start=k == 0, stop=k == KD - 1)
                mm.then_inc(s["f_z"], 1)
                pe.wait_ge(s["f_zq"], t + 1)
                for k in range(QT):
                    mm = pe.transpose(banks[3][:, k * P:(k + 1) * P], zq[:, k * P:(k + 1) * P], ident[:])
                mm.then_inc(s["f_qlt"], 1)
                pe.wait_ge(s["f_qlT"], t + 1)
                for b in range(2):
                    for k in range(QT):
                        mm = pe.matmul(banks[5 + b][:, 0:QL], qlT[:, k, :], w_q[:, k, b * QL:(b + 1) * QL],
                                       start=k == 0, stop=k == QT - 1)
                mm.then_inc(s["f_q"], 1)
                pe.wait_ge(s["f_c"], t + 1)
                for k in range(CT):
                    mm = pe.transpose(banks[4][:, k * P:(k + 1) * P], c_t[:, k * P:(k + 1) * P], ident[:])
                mm.then_inc(s["f_ct"], 1)
                pe.wait_ge(s["f_cT"], t + 1)
                pe.wait_ge(s["f_zck"], t + 1)
                for b, w in ((0, w_uk), (1, w_uv)):
                    for k in range(CT):
                        mm = pe.matmul(banks[b][:, :], cT[:, k, :], w[:, k, :], start=k == 0, stop=k == CT - 1)
                mm.then_inc(s["f_kv"], 1)
                pe.wait_ge(s["f_rot"], t + 1)
                pe.wait_ge(s["f_pin"], t + 1)
                for half, n in ((0, "f_tr0"), (1, "f_tr1")):
                    for i in range(H):
                        b = (2, 3, 4, 7)[2 * half + i // 4]
                        mm = pe.transpose(banks[b][0:HD, (i % 4) * P:(i % 4 + 1) * P], qk[:, half * H + i, :],
                                          ident[:])
                    mm.then_inc(s[n], 1)

        @block.scalar
        def _(act):
            act.wait_ge(s["f_consts"], 1)
            with act.Fori(0, TILES) as t:
                act.wait_ge(s["f_x_in"], 32 * t + 32)
                act.wait_ge(s["f_ssh"], t)
                act.wait_ge(s["f_rstd"], t)
                act.activation(junk[:, 0:D], x_t[:], ACT.Square, scale=D ** -0.5,
                               accum_out=ss[:]).then_inc(s["f_sqx"], 1)
                act.wait_ge(s["f_sqx"], t + 1)
                act.activation(ss[:], ss[:], ACT.Sqrt, bias=eps[:]).then_inc(s["f_std"], 1)
                act.wait_ge(s["f_rstd"], t + 1)
                act.wait_ge(s["f_z"], t + 1)
                act.activation(zq[:], banks[0][:, 0:QL], ACT.Copy, scale=rstd[:]).then_inc(s["f_zq"], 1)
                act.wait_ge(s["f_kr"], t)
                act.wait_ge(s["f_c"], t)
                act.activation(zck[:], banks[1][:, 0:KVL + ROPE], ACT.Copy, scale=rstd[:]).then_inc(s["f_zck"], 1)
                act.wait_ge(s["f_zck"], t + 1)
                act.wait_ge(s["f_zq"], t + 1)
                act.wait_ge(s["f_rstd2"], t)
                act.activation(junk[:, 0:QL], zq[:], ACT.Square, scale=QL ** -0.5,
                               accum_out=ss2[:, 0:1]).then_inc(s["f_ms"], 1)
                act.activation(junk[:, QL:QL + KVL], zck[:, 0:KVL], ACT.Square, scale=KVL ** -0.5,
                               accum_out=ss2[:, 1:2]).then_inc(s["f_ms"], 1)
                act.wait_ge(s["f_ms"], 2 * t + 2)
                act.activation(ss2[:], ss2[:], ACT.Sqrt, bias=eps[:]).then_inc(s["f_std2"], 1)
                act.wait_ge(s["f_qlt"], t + 1)
                act.activation(qlT[:], banks[3][:, 0:QL].rearrange("p (k t) -> p k t", k=QT),
                               ACT.Copy).then_inc(s["f_qlT"], 1)
                act.wait_ge(s["f_q"], t + 1)
                act.wait_ge(s["f_rstd2"], t + 1)
                act.wait_ge(s["f_tr0"], t)
                for b in range(2):
                    act.activation(qk[:, 4 * b:4 * b + 4, :],
                                   banks[5 + b][:, 0:QL].rearrange("p (h d) -> p h d", d=HD), ACT.Copy,
                                   scale=rstd2[:, 0:1]).then_inc(s["f_qev"], 1)
                act.wait_ge(s["f_kv"], t + 1)
                act.wait_ge(s["f_tr1"], t)
                act.activation(qk[:, H:2 * H, 0:NOPE], banks[0][:, :].rearrange("p (h d) -> p h d", d=NOPE),
                               ACT.Copy).then_inc(s["f_kev"], 1)
                act.wait_ge(s["f_kev"], t + 1)
                act.wait_ge(s["f_qev"], 2 * t + 2)
                act.wait_ge(s["f_kpe"], t + 1)
                act.activation(junk[:].rearrange("p (h d) -> p h d", d=HD), qk[:], ACT.Square,
                               scale=HD ** -0.5).then_inc(s["f_sqh"], 1)
                act.wait_ge(s["f_ssh"], t + 1)
                act.activation(ssh[:], ssh[:], ACT.Sqrt, bias=eps[:]).then_inc(s["f_stdh"], 1)
                act.wait_ge(s["f_tr0"], t + 1)
                for b in range(2):
                    mv = act.activation(qkT[0:HD, 4 * b:4 * b + 4, bass.ds(t * P, P)],
                                        banks[(2, 3)[b]][0:HD, :].rearrange("p (h t) -> p h t", t=P), ACT.Copy)
                mv.then_inc(s["f_ev0"], 1)
                act.wait_ge(s["f_tr1"], t + 1)
                for b in range(2):
                    mv = act.activation(qkT[0:HD, H + 4 * b:H + 4 * b + 4, bass.ds(t * P, P)],
                                        banks[(4, 7)[b]][0:HD, :].rearrange("p (h t) -> p h t", t=P), ACT.Copy)
                mv.then_inc(s["f_ev1"], 1)

        @block.vector
        def _(dve):
            dve.memset(eps[:], EPS).then_inc(s["f_consts"], 1)
            dve.wait_ge(s["f_wts"], 16 * 16)
            dve.tensor_tensor(w_in[:], w_in[:], g_attn[:].unsqueeze(2).to_broadcast((P, KD, IN_W)),
                              ALU.mult).then_inc(s["f_w_scaled"], 1)
            dve.tensor_tensor(w_q[:], w_q[:], g_ql[:].unsqueeze(2).to_broadcast((P, QT, H * HD)),
                              ALU.mult).then_inc(s["f_w_scaled"], 1)
            with dve.Fori(0, TILES) as t:
                rc = rope_c[:, bass.ds(t, 1), :]
                rs = rope_s[:, bass.ds(t, 1), :]
                dve.wait_ge(s["f_std"], t + 1)
                dve.wait_ge(s["f_zck"], t)
                dve.reciprocal(rstd[:], ss[:]).then_inc(s["f_rstd"], 1)
                dve.wait_ge(s["f_rstd"], t + 1)
                dve.wait_ge(s["f_z"], t + 1)
                dve.wait_ge(s["f_out"], 48 * t)
                dve.tensor_scalar(pin[:], banks[2][:, :], rstd[:], None, ALU.mult).then_inc(s["f_pin"], 1)
                dve.wait_ge(s["f_std2"], t + 1)
                dve.reciprocal(rstd2[:], ss2[:]).then_inc(s["f_rstd2"], 1)
                dve.wait_ge(s["f_rstd2"], t + 1)
                dve.scalar_tensor_tensor(out=c_t[:], in0=zck[:, 0:KVL], scalar=rstd2[:, 1:2], in1=g_kv[:],
                                         op0=ALU.mult, op1=ALU.mult).then_inc(s["f_c"], 1)
                dve.wait_ge(s["f_zck"], t + 1)
                dve.tensor_tensor(r_a[:, 0:1, :], zck[:, KVL:].unsqueeze(1), rc, ALU.mult).then_inc(s["f_ra"], 1)
                for i in range(2):
                    dve.tensor_tensor(r_b[:, 0:1, i * HALF:(i + 1) * HALF],
                                      zck[:, KVL + (1 - i) * HALF:KVL + (2 - i) * HALF].unsqueeze(1),
                                      rs[:, :, i * HALF:(i + 1) * HALF], ALU.mult).then_inc(s["f_rb"], 1)
                dve.wait_ge(s["f_ra"], t + 1)
                dve.wait_ge(s["f_rb"], 2 * t + 2)
                dve.tensor_tensor(kr[:], r_a[:, 0, :], r_b[:, 0, :], ALU.add).then_inc(s["f_kr"], 1)
                dve.wait_ge(s["f_ct"], t + 1)
                dve.tensor_copy(cT[:], banks[4][:, 0:KVL].rearrange("p (k t) -> p k t", k=CT)).then_inc(s["f_cT"], 1)
                dve.wait_ge(s["f_kr"], t + 1)
                dve.wait_ge(s["f_tr1"], t)
                dve.tensor_copy(qk[:, H:2 * H, NOPE:HD],
                                kr[:].unsqueeze(1).to_broadcast((P, H, ROPE))).then_inc(s["f_kpe"], 1)
                dve.wait_ge(s["f_kv"], t + 1)
                dve.tensor_copy(vall[:, bass.ds(t, 1), :], banks[1][:, :].unsqueeze(1)).then_inc(s["f_vev"], 1)
                dve.wait_ge(s["f_sqh"], t + 1)
                dve.tensor_reduce(ssh[:], junk[:].rearrange("p (h d) -> p h d", d=HD), AX,
                                  ALU.add).then_inc(s["f_ssh"], 1)
                dve.wait_ge(s["f_stdh"], t + 1)
                dve.reciprocal(rstdh[:], ssh[:]).then_inc(s["f_rstdh"], 1)
                dve.wait_ge(s["f_rstdh"], t + 1)
                dve.tensor_tensor(qk[:], qk[:], rstdh[:].unsqueeze(2).to_broadcast((P, 2 * H, HD)),
                                  ALU.mult).then_inc(s["f_n1"], 1)
                dve.wait_ge(s["f_n1"], t + 1)
                for i in range(2):
                    dve.tensor_tensor(qk[:, i * H:(i + 1) * H, :], qk[:, i * H:(i + 1) * H, :],
                                      g_qk[:, i:i + 1, :].to_broadcast((P, H, HD)), ALU.mult).then_inc(s["f_n2"], 1)
                dve.wait_ge(s["f_n2"], 2 * t + 2)
                dve.tensor_tensor(r_a[:], qk[:, 0:H, NOPE:HD], rc.to_broadcast((P, H, ROPE)),
                                  ALU.mult).then_inc(s["f_qra"], 1)
                for i in range(2):
                    dve.tensor_tensor(r_b[:, :, i * HALF:(i + 1) * HALF],
                                      qk[:, 0:H, NOPE + (1 - i) * HALF:NOPE + (2 - i) * HALF],
                                      rs[:, :, i * HALF:(i + 1) * HALF].to_broadcast((P, H, HALF)),
                                      ALU.mult).then_inc(s["f_qrb"], 1)
                dve.wait_ge(s["f_qra"], t + 1)
                dve.wait_ge(s["f_qrb"], 2 * t + 2)
                dve.tensor_tensor(qk[:, 0:H, NOPE:HD], r_a[:], r_b[:], ALU.add).then_inc(s["f_rot"], 1)


def prompt_attention(nc, a, qkT, vall):
    with ExitStack() as ctx:
        def sb(name, shape, dt=F32):
            return ctx.enter_context(nc.sbuf_tensor(name, shape, dt))

        ident = sb("a_ident", [P, P])
        causal = sb("a_causal", [P, P])
        q_now = [sb(f"a_q{e}", [HD, P]) for e in range(2)]
        prob = [sb(f"a_p{e}", [P, SEQ]) for e in range(2)]
        probT = [sb(f"a_pT{e}", [P, PT_TILES, P]) for e in range(2)]
        mx = [sb(f"a_mx{e}", [P, 1]) for e in range(2)]
        nmx = [sb(f"a_nmx{e}", [P, 1]) for e in range(2)]
        tot = [sb(f"a_tot{e}", [P, 1]) for e in range(2)]
        inv = [sb(f"a_inv{e}", [P, 1]) for e in range(2)]
        o_all = sb("a_o", [P, H * VD])
        oT = sb("a_oT", [P, G4, P])
        score = [ctx.enter_context(nc.psum_tensor(f"a_s{e}", [P, SEQ], F32)) for e in range(2)]
        turn = [ctx.enter_context(nc.psum_tensor(f"a_t{e}", [P, 512], F32)) for e in range(2)]
        out = [ctx.enter_context(nc.psum_tensor(f"a_op{e}", [P, 512], F32)) for e in range(2)]
        s = with_sems(nc, ctx, """a_in a_qc a_s a_mask a_mx a_nmx a_exp a_tr a_pt a_pv a_inv a_o a_ot a_otev
            a_st""")
        block = ctx.enter_context(nc.Block())
        PAIRS = H // 2

        def batches(i):
            return [range(b, min(b + 4, i + 1)) for b in range(0, i + 1, 4)]

        def batch_number(i, m, e, b):
            before = sum(H * len(batches(j)) for j in range(i))
            return before + (m * 2 + e) * len(batches(i)) + b

        @block.sync
        def _(sp):
            sp.dma_start(ident[:], a["ident"]).then_inc(s["a_in"], 16)
            sp.dma_start(causal[:], a["causal"]).then_inc(s["a_in"], 16)
            for i in range(PT_TILES):
                sp.wait_ge(s["a_otev"], i + 1)
                sp.dma_start(a["mixT_d"][:, :, i * P:(i + 1) * P], oT[:]).then_inc(s["a_st"], 16)
            sp.wait_ge(s["a_st"], 16 * PT_TILES)

        @block.tensor
        def _(pe):
            pe.wait_ge(s["a_in"], 32)
            for i in range(PT_TILES):
                L = (i + 1) * P
                after(pe, s["a_otev"], i)
                with pe.Fori(0, PAIRS) as m:
                    n = i * PAIRS + m
                    pe.wait_ge(s["a_exp"], 2 * n)
                    for e in range(2):
                        pe.wait_ge(s["a_qc"], 2 * n + e + 1)
                        for c in range(0, L, 512):
                            w = min(512, L - c)
                            mm = pe.matmul(score[e][:, c:c + w], q_now[e][:],
                                           qkT[0:HD, bass.ds(H + 2 * m + e, 1), c:c + w], start=True, stop=True)
                        mm.then_inc(s["a_s"], 1)
                    for e in range(2):
                        pe.wait_ge(s["a_exp"], 2 * n + e + 1)
                        for b, blocks in enumerate(batches(i)):
                            g = batch_number(i, m, e, b)
                            bank = (e * len(batches(i)) + b) % 2
                            pe.wait_ge(s["a_pt"], g if (e, b) == (0, 0) else g - 1)
                            for k in blocks:
                                mm = pe.transpose(turn[bank][:, (k % 4) * P:(k % 4 + 1) * P],
                                                  prob[e][:, k * P:(k + 1) * P], ident[:])
                            mm.then_inc(s["a_tr"], 1)
                    for e in range(2):
                        pe.wait_ge(s["a_pt"], batch_number(i, m, e, len(batches(i)) - 1) + 1)
                        pe.wait_ge(s["a_o"], 2 * n)
                        for k in range(i + 1):
                            mm = pe.matmul(out[e][:, 0:VD], probT[e][:, k, :],
                                           vall[:, k, bass.ds((2 * m + e) * VD, VD)], start=k == 0, stop=k == i)
                        mm.then_inc(s["a_pv"], 1)
                pe.wait_ge(s["a_o"], H * (i + 1))
                for k in range(G4):
                    mm = pe.transpose(score[0][:, k * P:(k + 1) * P], o_all[:, k * P:(k + 1) * P], ident[:])
                mm.then_inc(s["a_ot"], 1)

        @block.scalar
        def _(act):
            for i in range(PT_TILES):
                L = (i + 1) * P
                with act.Fori(0, PAIRS) as m:
                    n = i * PAIRS + m
                    act.wait_ge(s["a_s"], 2 * n)
                    for e in range(2):
                        act.activation(q_now[e][:], qkT[0:HD, bass.ds(2 * m + e, 1), i * P:(i + 1) * P],
                                       ACT.Copy).then_inc(s["a_qc"], 1)
                    for e in range(2):
                        act.wait_ge(s["a_nmx"], 2 * n + e + 1)
                        act.wait_ge(s["a_tr"], batch_number(i, m, 0, 0))
                        act.wait_ge(s["a_inv"], 2 * n)
                        act.activation(prob[e][:, 0:L], score[e][:, 0:L], ACT.Exp, bias=nmx[e][:], scale=SM,
                                       accum_out=tot[e][:]).then_inc(s["a_exp"], 1)
                    act.wait_ge(s["a_pv"], 2 * n)
                    for e in range(2):
                        for b, blocks in enumerate(batches(i)):
                            bank = (e * len(batches(i)) + b) % 2
                            act.wait_ge(s["a_tr"], batch_number(i, m, e, b) + 1)
                            act.activation(probT[e][:, 4 * b:4 * b + len(blocks), :],
                                           turn[bank][:, 0:len(blocks) * P].rearrange("p (k t) -> p k t", t=P),
                                           ACT.Copy).then_inc(s["a_pt"], 1)
                act.wait_ge(s["a_ot"], i + 1)
                after(act, s["a_st"], 16 * i)
                act.activation(oT[:], score[0][:, 0:512].rearrange("p (k t) -> p k t", t=P),
                               ACT.Copy).then_inc(s["a_otev"], 1)

        @block.vector
        def _(dve):
            dve.wait_ge(s["a_in"], 32)
            for i in range(PT_TILES):
                L = (i + 1) * P
                with dve.Fori(0, PAIRS) as m:
                    n = i * PAIRS + m
                    for e in range(2):
                        dve.wait_ge(s["a_s"], 2 * n + e + 1)
                        dve.tensor_tensor(score[e][:, L - P:L], score[e][:, L - P:L], causal[:],
                                          ALU.add).then_inc(s["a_mask"], 1)
                    for e in range(2):
                        dve.wait_ge(s["a_mask"], 2 * n + e + 1)
                        dve.tensor_reduce(mx[e][:], score[e][:, 0:L], AX, ALU.max).then_inc(s["a_mx"], 1)
                    dve.wait_ge(s["a_exp"], 2 * n)
                    for e in range(2):
                        dve.wait_ge(s["a_mx"], 2 * n + e + 1)
                        dve.tensor_scalar(nmx[e][:], mx[e][:], -SM, None, ALU.mult).then_inc(s["a_nmx"], 1)
                    dve.wait_ge(s["a_o"], 2 * n)
                    for e in range(2):
                        dve.wait_ge(s["a_exp"], 2 * n + e + 1)
                        dve.reciprocal(inv[e][:], tot[e][:]).then_inc(s["a_inv"], 1)
                    if i:
                        dve.wait_ge(s["a_ot"], i)
                    for e in range(2):
                        dve.wait_ge(s["a_inv"], 2 * n + e + 1)
                        dve.wait_ge(s["a_pv"], 2 * n + e + 1)
                        dve.tensor_scalar(o_all[:, bass.ds((2 * m + e) * VD, VD)], out[e][:, 0:VD], inv[e][:], None,
                                          ALU.mult).then_inc(s["a_o"], 1)


def sample_attention(nc, a, qkT):
    SQ = DEC_S * H
    with ExitStack() as ctx:
        def sb(name, shape, dt=F32):
            return ctx.enter_context(nc.sbuf_tensor(name, shape, dt))

        ident = sb("d_ident", [P, P])
        w_uk = sb("d_w_uk", [P, CT, H * NOPE])
        w_uv = sb("d_w_uv", [P, CT, H * VD])
        w_ukT = sb("d_w_ukT", [NOPE, H, KVL])
        g_k = sb("d_g_k", [HD, 1])
        newmask = sb("d_newmask", [DEC_S, H, DEC_S])
        table = sb("d_table", [1, DEC_B * PAGES], I32)
        eps = sb("d_eps", [P, 1])
        qg = sb("d_qg", [NOPE, H, NS])
        qr = sb("d_qr", [ROPE, H, NS])
        qa = sb("d_qa", [P, CT, H, NS])
        page = [sb(f"d_page{e}", [P, PAGES, 2 * KVL + ROPE]) for e in range(2)]
        krT = [sb(f"d_krT{e}", [ROPE, PAGES, P]) for e in range(2)]
        k_new = sb("d_k_new", [HD, H, DEC_S])
        c_now = [sb(f"d_c_now{e}", [DEC_S, KVL]) for e in range(2)]
        sq = [sb(f"d_sq{e}", [P, H * NOPE]) for e in range(2)]
        krsq = sb("d_krsq", [P, PAGES, ROPE])
        krss = sb("d_krss", [P, PAGES])
        kss2 = [sb(f"d_kss{e}", [P, PAGES, H]) for e in range(2)]
        s_all2 = [sb(f"d_s{e}", [P, PAGES + 1, SQ]) for e in range(2)]
        rows = sb("d_rows", [P, PAST + DEC_S])
        s_row = rows[0:SQ, :]
        mx = sb("d_mx", [SQ, 1])
        nmx = sb("d_nmx", [SQ, 1])
        tot = sb("d_tot", [SQ, 1])
        inv = sb("d_inv", [SQ, 1])
        pT = sb("d_pT", [P, PAGES + 1, SQ])
        ol = sb("d_ol", [SQ, KVL])
        olT = sb("d_olT", [P, CT, H, NS])
        o = rows[0:NS, 0:H * VD]
        oT = rows[:, 512:512 + G4 * P].rearrange("p (k t) -> p k t", k=G4)
        bank = lambda n: ctx.enter_context(nc.psum_tensor(n, [P, 512], F32))
        kn = [bank("d_kn0"), bank("d_kn1")]
        st = [bank("d_st0"), bank("d_st1")]
        misc = [bank("d_m0"), bank("d_m1")]
        new = bank("d_new")
        lat = bank("d_lat")
        s = with_sems(nc, ctx, """d_tab d_in d_wuv d_pg0 d_pg1 d_eps d_qg d_qap d_qa d_mm d_sq d_red d_sev d_krsq d_krss
            d_ks1 d_ks2 d_ks3 d_s1 d_knew d_new d_smask d_tr d_row d_mx d_nmx d_exp d_inv d_ptr d_pt d_lat d_ol
            d_olt d_olT d_op d_o d_ot d_zero d_oT d_st""")
        loaded = [s["d_pg0"], s["d_pg1"]]
        LOADS = 2 * PAGES + 1
        n_phys = a["page"].shape[0]
        block = ctx.enter_context(nc.Block())

        def sequences(eng, begin, pages, tail):
            def one(b, e, n, t):
                begin(b, e, n)
                pages(b, e, {} if t is None else tail(t, 1 - e))
            one(0, 0, 1, None)
            with eng.Fori(0, DEC_B // 2 - 1) as m:
                one(2 * m + 1, 1, m + 1, 2 * m)
                one(2 * m + 2, 0, m + 2, 2 * m + 1)
            one(DEC_B - 1, 1, DEC_B // 2, DEC_B - 2)
            for step in tail(DEC_B - 1, 1).values():
                step()

        @block.sync
        def _(sp):
            sp.dma_start(table[:], a["page_table"].rearrange("b p -> (b p)").unsqueeze(0)).then_inc(s["d_tab"], 16)
            for dst, src in ((w_ukT, a["w_ukT"]), (g_k, a["g_k_col"]), (w_uk, a["w_uk"]), (ident, a["ident"]),
                             (newmask, a["newmask"])):
                sp.dma_start(dst[:], src).then_inc(s["d_in"], 16)
            sp.wait_ge(s["d_tab"], 16)

            def load(b, e):
                sp.dma_start(c_now[e][:], a["kv_all"][bass.ds(SEQ + b * DEC_S, DEC_S), :]).then_inc(loaded[e], 16)
                for p in range(PAGES):
                    phys = sp.value_load(table[0:1, bass.ds(b * PAGES + p, 1)], min_val=0, max_val=n_phys - 1)
                    sp.dma_start(page[e][:, p, :],
                                 a["page"][bass.ds(phys, 1)].rearrange("o p c -> (o p) c")).then_inc(loaded[e], 16)
                    sp.dma_start(krT[e][:, p, :],
                                 a["page_krT"][bass.ds(phys, 1)].rearrange("o p c -> (o p) c")).then_inc(loaded[e], 16)
            load(0, 0)
            load(1, 1)
            sp.dma_start(w_uv[:], a["w_uv"]).then_inc(s["d_wuv"], 16)
            with sp.Fori(0, DEC_B // 2 - 1) as m:
                for e in range(2):
                    sp.wait_ge(s["d_lat"], 2 * m + e + 1)
                    load(2 * m + e + 2, e)
            sp.wait_ge(s["d_oT"], 1)
            sp.dma_start(a["mixT_d"][:, :, SEQ:NPAD], oT).then_inc(s["d_st"], 16)
            sp.wait_ge(s["d_st"], 16)

        @block.tensor
        def _(pe):
            pe.wait_ge(s["d_in"], 16 * 5)
            pe.wait_ge(s["d_qg"], 2)
            for k in range(CT):
                for h in range(H):
                    mm = pe.matmul(kn[k][:, h * NS:(h + 1) * NS], w_ukT[:, h, k * P:(k + 1) * P], qg[:, h, :],
                                   start=True, stop=True)
            mm.then_inc(s["d_qap"], 1)
            pe.wait_ge(s["d_qa"], 2)

            def begin(b, e, n):
                pe.wait_ge(loaded[e], 16 * LOADS * n)

            def pages(b, e, tail):
                cols = bass.ds(b * DEC_S, DEC_S)
                for p in range(PAGES):
                    after(pe, s["d_sq"], b * PAGES + p - 1)
                    after(pe, s["d_sev"], b * PAGES + p - 1)
                    for k in range(CT):
                        pe.matmul(kn[p % 2][:, :], page[e][:, p, k * P:(k + 1) * P], w_uk[:, k, :],
                                  start=k == 0, stop=k == CT - 1)
                    for k in range(CT):
                        pe.matmul(st[p % 2][:, 0:SQ].rearrange("p (h t) -> p h t", t=DEC_S),
                                  page[e][:, p, k * P:(k + 1) * P], qa[:, k, :, cols], start=k == 0, stop=False)
                    mm = pe.matmul(st[p % 2][:, 0:SQ].rearrange("p (h t) -> p h t", t=DEC_S),
                                   krT[e][:, p, :], qr[:, :, cols], start=False, stop=True)
                    mm.then_inc(s["d_mm"], 1)
                    if p == 0:
                        pe.wait_ge(s["d_knew"], b + 1)
                        after(pe, s["d_smask"], b)
                        for h in range(H):
                            mm = pe.matmul(new[0:DEC_S, h * DEC_S:(h + 1) * DEC_S], k_new[:, h, :],
                                           qkT[0:HD, h, bass.ds(SEQ + b * DEC_S, DEC_S)], start=True, stop=True)
                        mm.then_inc(s["d_new"], 1)
                    if p in tail:
                        tail[p]()

            def tail(t, e):
                s_all = s_all2[e]

                def turn_first():
                    pe.wait_ge(s["d_s1"], t + 1)
                    pe.wait_ge(s["d_smask"], t + 1)
                    pe.wait_ge(s["d_olT"], t)
                    pe.wait_ge(s["d_pt"], 2 * t)
                    turn(0)
                    turn(1)

                def turn(c):
                    for p in range(4 * c, 4 * c + 4):
                        mm = pe.transpose(misc[c % 2][0:SQ, (p % 4) * P:(p % 4 + 1) * P], s_all[:, p, :], ident[:])
                    mm.then_inc(s["d_tr"], 1)

                def turn_rest():
                    for c in (2, 3):
                        pe.wait_ge(s["d_row"], 5 * t + c - 1)
                        turn(c)
                    pe.transpose(new[0:SQ, 2 * SQ:2 * SQ + DEC_S], s_all[0:DEC_S, PAGES, :],
                                 ident[0:DEC_S, 0:DEC_S]).then_inc(s["d_tr"], 1)

                def probs():
                    pe.wait_ge(s["d_exp"], t + 1)
                    for p in range(PAGES):
                        mm = pe.matmul(misc[0][:, p * SQ:(p + 1) * SQ], s_row[:, p * P:(p + 1) * P],
                                       ident[0:SQ, 0:SQ], start=True, stop=True)
                    mm.then_inc(s["d_ptr"], 1)
                    pe.transpose(misc[1][0:DEC_S, 0:SQ], s_row[:, PAST:PAST + DEC_S],
                                 ident[0:SQ, 0:SQ]).then_inc(s["d_ptr"], 1)

                def latent():
                    pe.wait_ge(s["d_pt"], 2 * t + 2)
                    for p in range(PAGES):
                        pe.matmul(lat[0:SQ, 0:KVL], pT[:, p, :], page[e][:, p, KVL:2 * KVL], start=p == 0, stop=False)
                    pe.matmul(lat[0:SQ, 0:KVL], pT[0:DEC_S, PAGES, :], c_now[e][:], start=False,
                              stop=True).then_inc(s["d_lat"], 1)

                def latent_turn():
                    pe.wait_ge(s["d_ol"], t + 1)
                    for k in range(CT):
                        mm = pe.matmul(misc[0][:, k * SQ:(k + 1) * SQ], ol[:, k * P:(k + 1) * P],
                                       ident[0:SQ, 0:SQ], start=True, stop=True)
                    mm.then_inc(s["d_olt"], 1)
                return {1: turn_first, 2: turn_rest, 5: probs, 6: latent, 7: latent_turn}
            sequences(pe, begin, pages, tail)
            pe.wait_ge(s["d_wuv"], 16)
            pe.wait_ge(s["d_olT"], DEC_B)
            for h in range(H):
                for k in range(CT):
                    mm = pe.matmul(lat[0:NS, h * VD:(h + 1) * VD], olT[:, k, h, :], w_uv[:, k, h * VD:(h + 1) * VD],
                                   start=k == 0, stop=k == CT - 1)
            mm.then_inc(s["d_op"], 1)
            pe.wait_ge(s["d_o"], 1)
            for k in range(G4):
                mm = pe.transpose(new[:, k * NS:(k + 1) * NS], o[:, k * P:(k + 1) * P], ident[0:NS, 0:NS])
            mm.then_inc(s["d_ot"], 1)

        @block.scalar
        def _(act):
            act.wait_ge(s["d_eps"], 1)
            act.wait_ge(s["d_qap"], 1)
            for k in range(CT):
                act.activation(qa[:, k, :, :], kn[k][:, 0:H * NS].rearrange("p (h t) -> p h t", t=NS),
                               ACT.Copy).then_inc(s["d_qa"], 1)

            def begin(b, e, n):
                act.wait_ge(loaded[e], 16 * LOADS * n)
                after(act, s["d_krss"], b)
                act.activation(krsq[:], page[e][:, :, 2 * KVL:], ACT.Square,
                               scale=HD ** -0.5).then_inc(s["d_krsq"], 1)

            def pages(b, e, tail):
                for p in range(PAGES):
                    if p in tail:
                        tail[p]()
                    act.wait_ge(s["d_mm"], b * PAGES + p + 1)
                    after(act, s["d_red"], b * PAGES + p - 1)
                    act.activation(sq[p % 2][:], kn[p % 2][:, :], ACT.Square,
                                   scale=HD ** -0.5).then_inc(s["d_sq"], 1)
                act.wait_ge(s["d_ks1"], b + 1)
                act.activation(kss2[e][:], kss2[e][:], ACT.Sqrt, bias=eps[:]).then_inc(s["d_ks2"], 1)

            def tail(t, e):
                def row(c):
                    act.wait_ge(s["d_tr"], 5 * t + c + 1)
                    if c == 0:
                        act.wait_ge(s["d_ptr"], 2 * t)
                    w = 512 if c < 4 else DEC_S
                    act.activation(s_row[:, 512 * c:512 * c + w],
                                   misc[c % 2][0:SQ, 0:w] if c < 4 else new[0:SQ, 2 * SQ:2 * SQ + w],
                                   ACT.Copy).then_inc(s["d_row"], 1)

                def rows_first():
                    row(0)
                    row(1)

                def rows_rest():
                    for c in (2, 3, 4):
                        row(c)

                def exp():
                    act.wait_ge(s["d_row"], 5 * t + 5)
                    act.wait_ge(s["d_nmx"], t + 1)
                    act.wait_ge(s["d_inv"], t)
                    act.activation(s_row, s_row, ACT.Exp, bias=nmx[:], scale=SM,
                                   accum_out=tot[:]).then_inc(s["d_exp"], 1)

                def probs():
                    act.wait_ge(s["d_lat"], t)
                    act.wait_ge(s["d_ptr"], 2 * t + 1)
                    act.activation(pT[:, 0:PAGES, :], misc[0][:, :].rearrange("p (k t) -> p k t", t=SQ),
                                   ACT.Copy).then_inc(s["d_pt"], 1)
                    act.wait_ge(s["d_ptr"], 2 * t + 2)
                    act.activation(pT[0:DEC_S, PAGES, :], misc[1][0:DEC_S, 0:SQ], ACT.Copy).then_inc(s["d_pt"], 1)

                def latent_turn():
                    act.wait_ge(s["d_olt"], t + 1)
                    act.activation(olT[:, :, :, bass.ds(t * DEC_S, DEC_S)],
                                   misc[0][:, 0:CT * SQ].rearrange("p (k h t) -> p k h t", k=CT, h=H),
                                   ACT.Copy).then_inc(s["d_olT"], 1)
                return {2: rows_first, 3: rows_rest, 5: exp, 6: probs, 8: latent_turn}
            sequences(act, begin, pages, tail)
            act.wait_ge(s["d_op"], 1)
            act.activation(o, lat[0:NS, :], ACT.Copy).then_inc(s["d_o"], 1)
            act.wait_ge(s["d_ot"], 1)
            act.wait_ge(s["d_zero"], 1)
            act.activation(oT[:, :, 0:NS], new[:, 0:G4 * NS].rearrange("p (k t) -> p k t", t=NS),
                           ACT.Copy).then_inc(s["d_oT"], 1)

        @block.vector
        def _(dve):
            dve.memset(eps[:], EPS).then_inc(s["d_eps"], 1)
            dve.wait_ge(s["d_in"], 16 * 5)
            dve.tensor_scalar(qg[:], qkT[0:NOPE, 0:H, SEQ:NT], g_k[0:NOPE, :], None, ALU.mult).then_inc(s["d_qg"], 1)
            dve.tensor_scalar(qr[:], qkT[NOPE:HD, 0:H, SEQ:NT], g_k[NOPE:HD, :], None,
                              ALU.mult).then_inc(s["d_qg"], 1)

            def begin(b, e, n):
                after(dve, s["d_new"], b)
                dve.tensor_copy(k_new[:], qkT[0:HD, H:2 * H, bass.ds(SEQ + b * DEC_S, DEC_S)]).then_inc(s["d_knew"], 1)
                dve.wait_ge(s["d_krsq"], b + 1)
                after(dve, s["d_ks1"], b)
                dve.tensor_reduce(krss[:], krsq[:], AX, ALU.add).then_inc(s["d_krss"], 1)
                after(dve, s["d_tr"], 5 * (b - 1))

            def pages(b, e, tail):
                kss, s_all = kss2[e], s_all2[e]
                for p in range(PAGES):
                    if p in tail:
                        tail[p]()
                    dve.wait_ge(s["d_mm"], b * PAGES + p + 1)
                    dve.tensor_copy(s_all[:, p, :], st[p % 2][:, 0:SQ]).then_inc(s["d_sev"], 1)
                    dve.wait_ge(s["d_sq"], b * PAGES + p + 1)
                    dve.tensor_reduce(kss[:, p, :], sq[p % 2][:].rearrange("p (h n) -> p h n", n=NOPE), AX,
                                      ALU.add).then_inc(s["d_red"], 1)
                dve.wait_ge(s["d_red"], (b + 1) * PAGES)
                dve.wait_ge(s["d_krss"], b + 1)
                dve.tensor_tensor(kss[:], kss[:], krss[:].unsqueeze(2).to_broadcast((P, PAGES, H)),
                                  ALU.add).then_inc(s["d_ks1"], 1)
                dve.wait_ge(s["d_new"], b + 1)
                dve.tensor_tensor(s_all[0:DEC_S, PAGES, :].rearrange("p (h t) -> p h t", t=DEC_S),
                                  new[0:DEC_S, 0:SQ].rearrange("p (h t) -> p h t", t=DEC_S), newmask[:],
                                  ALU.add).then_inc(s["d_smask"], 1)
                dve.wait_ge(s["d_ks2"], b + 1)
                dve.reciprocal(kss[:], kss[:]).then_inc(s["d_ks3"], 1)
                dve.wait_ge(s["d_ks3"], b + 1)
                dve.wait_ge(s["d_sev"], (b + 1) * PAGES)
                sv = s_all[:, 0:PAGES, :].rearrange("p k (h t) -> p (k h) t", t=DEC_S)
                dve.tensor_tensor(sv, sv, kss[:].rearrange("p k h -> p (k h)").unsqueeze(2)
                                  .to_broadcast((P, PAGES * H, DEC_S)), ALU.mult).then_inc(s["d_s1"], 1)

            def tail(t, e):
                def maximum():
                    dve.wait_ge(s["d_row"], 5 * t + 5)
                    dve.tensor_reduce(mx[:], s_row, AX, ALU.max).then_inc(s["d_mx"], 1)
                    dve.wait_ge(s["d_mx"], t + 1)
                    dve.wait_ge(s["d_exp"], t)
                    dve.tensor_scalar(nmx[:], mx[:], -SM, None, ALU.mult).then_inc(s["d_nmx"], 1)

                def latent():
                    dve.wait_ge(s["d_exp"], t + 1)
                    dve.reciprocal(inv[:], tot[:]).then_inc(s["d_inv"], 1)
                    dve.wait_ge(s["d_inv"], t + 1)
                    dve.wait_ge(s["d_lat"], t + 1)
                    dve.wait_ge(s["d_olt"], t)
                    dve.tensor_scalar(ol[:], lat[0:SQ, 0:KVL], inv[:], None, ALU.mult).then_inc(s["d_ol"], 1)
                return {4: maximum, 7: latent}
            sequences(dve, begin, pages, tail)
            dve.wait_ge(s["d_ptr"], 2 * DEC_B)
            dve.memset(oT, 0.0).then_inc(s["d_zero"], 1)


def mixer_out(nc, a):
    with ExitStack() as ctx:
        def sb(name, shape, dt=F32):
            return ctx.enter_context(nc.sbuf_tensor(name, shape, dt))

        ident = sb("o_ident", [P, P])
        band = sb("o_band", [P, 5, G4, P])
        w_pool = sb("o_w_pool", [P, G4, P])
        scale = sb("o_scale", [P, G4])
        w_o = sb("o_w_o", [P, KD, D])
        g_ffn = sb("o_g_ffn", [P, KD])
        eps = sb("o_eps", [P, 1])
        x_t = sb("o_x", [P, D])
        rows_now = sb("o_rows", [P, PW])
        rows_old = sb("o_rows_old", [P, PW])
        mT = sb("o_mT", [P, KD, P])
        pooled = sb("o_pooled", [P, G4, P])
        x1 = sb("o_x1", [P, D])
        h2 = sb("o_h2", [P, D])
        h2T = sb("o_h2T", [P, KD, P])
        ss = sb("o_ss", [P, 1])
        rstd = sb("o_rstd", [P, 1])
        bank = lambda n: ctx.enter_context(nc.psum_tensor(n, [P, 512], F32))
        pool_b, mix_b = bank("o_pb"), bank("o_mb")
        out_b = [bank("o_o0"), bank("o_o1")]
        turn_b = [bank("o_t0"), bank("o_t1")]
        s = with_sems(nc, ctx, """o_wts o_eps o_in o_pl o_plev o_y o_yev o_mm o_x1 o_sq o_std o_rstd o_h2 o_tr
            o_h2T o_st o_pool""")
        block = ctx.enter_context(nc.Block())

        @block.sync
        def _(sp):
            for dst, src in ((ident, "ident"), (band, "band"), (w_pool, "w_pool"), (scale, "pool_scale"),
                             (w_o, "w_o"), (g_ffn, "g_ffn")):
                sp.dma_start(dst[:], a[src]).then_inc(s["o_wts"], 16)
            sp.dma_start(a["pool_prompt"], a["pin_d"][SEQ - PSTATE:SEQ, :]).then_inc(s["o_pool"], 16)
            sp.dma_start(a["pool_sample"][:, 0:PSTATE - DEC_S, :],
                         a["state_pool"][:, DEC_S:PSTATE, :]).then_inc(s["o_pool"], 16)
            sp.dma_start(a["pool_sample"][:, PSTATE - DEC_S:PSTATE, :],
                         a["pin_d"][SEQ:NT, :].rearrange("(b t) c -> b t c", t=DEC_S)).then_inc(s["o_pool"], 16)

            def tile(t, old):
                at = t * P
                after(sp, s["o_x1"], 2 * t)
                sp.dma_start(rows_now[:], a["pin_d"][bass.ds(at, P), :]).then_inc(s["o_in"], 16)
                sp.dma_start(rows_old[:], old).then_inc(s["o_in"], 16)
                sp.dma_start(mT[:, 0:G4, :], a["mixT_d"][:, :, bass.ds(at, P)]).then_inc(s["o_in"], 16)
                sp.dma_start(x_t[:], a["x"][bass.ds(at, P), :]).then_inc(s["o_in"], 16)

            def store(t, n):
                sp.wait_ge(s["o_h2T"], 2 * t + 2)
                sp.dma_start(a["x1_d"][bass.ds(t * P, P), :], x1[:]).then_inc(s["o_st"], 16)
                sp.dma_start(a["h2T_d"][:, :, bass.ds(t * P, n)], h2T[:, :, 0:n]).then_inc(s["o_st"], 16)
            tile(0, a["state"])
            with sp.Fori(0, PT_TILES - 1) as t:
                tile(t + 1, a["pin_d"][bass.ds(t * P, P), :])
                store(t, P)
            tile(PT_TILES, a["state"])
            store(PT_TILES - 1, P)
            store(PT_TILES, NS)
            sp.wait_ge(s["o_st"], 32 * TILES)
            sp.wait_ge(s["o_pool"], 48)

        @block.tensor
        def _(pe):
            pe.wait_ge(s["o_wts"], 96)

            def tile(t, now, old):
                pe.wait_ge(s["o_in"], 64 * t + 64)
                after(pe, s["o_plev"], t)
                for g in range(G4):
                    mm = pe.matmul(pool_b[:, g * P:(g + 1) * P], rows_now[:, g * P:(g + 1) * P], band[:, now, g, :],
                                   start=True, stop=old is None)
                    if old is not None:
                        mm = pe.matmul(pool_b[:, g * P:(g + 1) * P], rows_old[:, g * P:(g + 1) * P],
                                       band[:, old, g, :], start=False, stop=True)
                mm.then_inc(s["o_pl"], 1)
                pe.wait_ge(s["o_plev"], t + 1)
                after(pe, s["o_yev"], t)
                for g in range(G4):
                    mm = pe.matmul(mix_b[:, g * P:(g + 1) * P], w_pool[:, g, :], pooled[:, g, :], start=True,
                                   stop=True)
                mm.then_inc(s["o_y"], 1)
                pe.wait_ge(s["o_yev"], t + 1)
                after(pe, s["o_x1"], 2 * t)
                for n in range(2):
                    for k in range(KD):
                        mm = pe.matmul(out_b[n][:, :], mT[:, k, :], w_o[:, k, n * 512:(n + 1) * 512], start=k == 0,
                                       stop=k == KD - 1)
                mm.then_inc(s["o_mm"], 1)
                pe.wait_ge(s["o_h2"], t + 1)
                after(pe, s["o_h2T"], 2 * t)
                for k in range(KD):
                    mm = pe.transpose(turn_b[k // 4][:, (k % 4) * P:(k % 4 + 1) * P], h2[:, k * P:(k + 1) * P],
                                      ident[:])
                mm.then_inc(s["o_tr"], 1)
            tile(0, 0, None)
            with pe.Fori(1, PT_TILES) as t:
                tile(t, 1, 2)
            tile(PT_TILES, 3, 4)

        @block.scalar
        def _(act):
            act.wait_ge(s["o_eps"], 1)
            with act.Fori(0, TILES) as t:
                act.wait_ge(s["o_pl"], t + 1)
                act.wait_ge(s["o_y"], t)
                act.activation(pooled[:], pool_b[:, :].rearrange("p (g t) -> p g t", g=G4),
                               ACT.Copy).then_inc(s["o_plev"], 1)
                act.wait_ge(s["o_x1"], 2 * t + 2)
                act.wait_ge(s["o_rstd"], t)
                act.wait_ge(s["o_tr"], t)
                act.activation(h2[:], x1[:], ACT.Square, scale=D ** -0.5, accum_out=ss[:]).then_inc(s["o_sq"], 1)
                act.wait_ge(s["o_sq"], t + 1)
                act.activation(ss[:], ss[:], ACT.Sqrt, bias=eps[:]).then_inc(s["o_std"], 1)
                act.wait_ge(s["o_rstd"], t + 1)
                act.activation(h2[:], x1[:], ACT.Copy, scale=rstd[:]).then_inc(s["o_h2"], 1)

        @block.vector
        def _(dve):
            dve.memset(eps[:], EPS).then_inc(s["o_eps"], 1)
            dve.wait_ge(s["o_wts"], 96)
            with dve.Fori(0, TILES) as t:
                dve.wait_ge(s["o_y"], t + 1)
                dve.tensor_tensor(mT[:, G4:KD, :], mix_b[:, :].rearrange("p (g t) -> p g t", g=G4),
                                  scale[:].unsqueeze(2).to_broadcast((P, G4, P)), ALU.mult).then_inc(s["o_yev"], 1)
                dve.wait_ge(s["o_mm"], t + 1)
                dve.wait_ge(s["o_st"], 32 * t)
                dve.wait_ge(s["o_h2"], t)
                for n in range(2):
                    dve.tensor_tensor(x1[:, n * 512:(n + 1) * 512], out_b[n][:, :], x_t[:, n * 512:(n + 1) * 512],
                                      ALU.add).then_inc(s["o_x1"], 1)
                dve.wait_ge(s["o_std"], t + 1)
                dve.reciprocal(rstd[:], ss[:]).then_inc(s["o_rstd"], 1)
                dve.wait_ge(s["o_tr"], t + 1)
                for n in range(2):
                    dve.tensor_tensor(h2T[:, 4 * n:4 * n + 4, :],
                                      turn_b[n][:, :].rearrange("p (g t) -> p g t", g=4),
                                      g_ffn[:, 4 * n:4 * n + 4].unsqueeze(2).to_broadcast((P, 4, P)),
                                      ALU.mult).then_inc(s["o_h2T"], 1)


def router(nc, a, h2, picks):
    with ExitStack() as ctx:
        def sb(name, shape, dt=F32):
            return ctx.enter_context(nc.sbuf_tensor(name, shape, dt))

        ident = sb("r_ident", [P, P])
        iota = sb("r_iota", [P, P])
        scores = sb("r_scores", [P, TILES, HP, NK])
        route_scores(nc, a, h2, ident, iota, scores)
        choose(nc, ident, iota, scores, picks)


def route_scores(nc, a, h2, ident, iota, scores):
    h2h, h2l = h2
    with ExitStack() as ctx:
        def sb(name, shape, dt=F32):
            return ctx.enter_context(nc.sbuf_tensor(name, shape, dt))

        keysT = sb("r_keysT", [P, HP, NK])
        w = [sb(f"r_w{e}", [P, KD, P]) for e in range(2)]
        wh = [sb(f"r_wh{e}", [P, KD, P], F32R) for e in range(2)]
        wl = [sb(f"r_wl{e}", [P, KD, P], F32R) for e in range(2)]
        qT = [sb(f"r_qT{e}", [P, NT]) for e in range(2)]
        part = [sb(f"r_part{e}", [P, NT]) for e in range(2)]
        bank = lambda n: ctx.enter_context(nc.psum_tensor(n, [P, 512], F32))
        q_b = [bank("r_q0"), bank("r_q1")]
        s_b = [bank(f"r_s{c}") for c in range(3)]
        s = with_sems(nc, ctx, """r_in r_hin0 r_hin1 r_hh r_hl r_win0 r_win1 r_wh r_wl r_q r_qev r_s r_sev
            r_zero""")
        w_in = [s["r_win0"], s["r_win1"]]
        h_in = [s["r_hin0"], s["r_hin1"]]
        with nc.Block() as block:
            @block.sync
            def _(sp):
                for dst, src in ((keysT, "keysT"), (ident, "ident"), (iota, "iota")):
                    sp.dma_start(dst[:], a[src]).then_inc(s["r_in"], 16)
                for k in range(KD):
                    if k >= 2:
                        sp.wait_ge(s["r_hl"], k - 1)
                    sp.dma_start(part[k % 2][:], a["h2T_d"][:, k, :]).then_inc(h_in[k % 2], 16)
                with sp.Fori(0, HP // 2) as m:
                    for e in range(2):
                        sp.wait_ge(s["r_wl"], 2 * m)
                        sp.dma_start(w[e][:], a["w_pq"][bass.ds(2 * m + e, 1)].rearrange("o p k c -> (o p) k c")
                                     ).then_inc(w_in[e], 16)

            @block.tensor
            def _(pe):
                pe.wait_ge(s["r_in"], 48)
                pe.wait_ge(s["r_hl"], KD)
                pe.wait_ge(s["r_hh"], KD)
                with pe.Fori(0, HP // 2) as m:
                    for e in range(2):
                        j = 2 * m + e
                        pe.wait_ge(s["r_wl"], j + 1)
                        for b in range(3):
                            pe.wait_ge(s["r_qev"], 6 * m + max(3 * e + b - 1, 0))
                            cols = slice(b * TB, (b + 1) * TB)
                            o = q_b[(3 * e + b) % 2][:, 0:TB]
                            for k in range(KD):
                                pe.matmul(o, wh[e][:, k, :], h2h[:, k, cols], start=k == 0, stop=False)
                                pe.matmul(o, wh[e][:, k, :], h2l[:, k, cols], start=False, stop=False)
                                mm = pe.matmul(o, wl[e][:, k, :], h2h[:, k, cols], start=False, stop=k == KD - 1)
                            mm.then_inc(s["r_q"], 1)
                        pe.wait_ge(s["r_qev"], 3 * j + 3)
                        pe.wait_ge(s["r_sev"], 3 * j)
                        for t in range(TILES):
                            n = P if t < PT_TILES else NS
                            mm = pe.matmul(s_b[t // 4][0:n, (t % 4) * NK:(t % 4 + 1) * NK], qT[e][:, t * P:t * P + n],
                                           keysT[:, bass.ds(j, 1), :], start=True, stop=True)
                        mm.then_inc(s["r_s"], 1)

            @block.scalar
            def _(act):
                for k in range(KD):
                    act.wait_ge(h_in[k % 2], 16 * (k // 2 + 1))
                    act.activation(h2h[:, k, :], part[k % 2][:], ACT.Copy).then_inc(s["r_hh"], 1)
                with act.Fori(0, HP // 2) as m:
                    for e in range(2):
                        j = 2 * m + e
                        act.wait_ge(w_in[e], 16 * m + 16)
                        act.wait_ge(s["r_q"], 6 * m)
                        act.activation(wh[e][:], w[e][:], ACT.Copy).then_inc(s["r_wh"], 1)
                    for e in range(2):
                        j = 2 * m + e
                        for b in range(3):
                            act.wait_ge(s["r_q"], 3 * j + b + 1)
                            act.wait_ge(s["r_s"], 2 * m)
                            act.activation(qT[e][:, b * TB:(b + 1) * TB], q_b[(3 * e + b) % 2][:, 0:TB],
                                           ACT.Copy).then_inc(s["r_qev"], 1)

            @block.vector
            def _(dve):
                dve.memset(scores[:, PT_TILES, :, :], 0.0).then_inc(s["r_zero"], 1)
                dve.wait_ge(s["r_zero"], 1)
                for k in range(KD):
                    dve.wait_ge(h_in[k % 2], 16 * (k // 2 + 1))
                    dve.wait_ge(s["r_hh"], k + 1)
                    dve.tensor_tensor(h2l[:, k, :], part[k % 2][:], h2h[:, k, :].bitcast(F32),
                                      ALU.subtract).then_inc(s["r_hl"], 1)
                with dve.Fori(0, HP // 2) as m:
                    for e in range(2):
                        dve.wait_ge(s["r_wh"], 2 * m + e + 1)
                        dve.tensor_tensor(wl[e][:], w[e][:], wh[e][:].bitcast(F32), ALU.subtract).then_inc(s["r_wl"], 1)
                    for e in range(2):
                        j = 2 * m + e
                        dve.wait_ge(s["r_s"], j + 1)
                        for c in range(2):
                            dve.tensor_copy(scores[:, 4 * c:4 * c + 4, bass.ds(j, 1), :],
                                            s_b[c][:, :].rearrange("p (t o n) -> p t o n", t=4, o=1)
                                            ).then_inc(s["r_sev"], 1)
                        dve.tensor_copy(scores[0:NS, PT_TILES, bass.ds(j, 1), :],
                                        s_b[2][0:NS, 0:NK].unsqueeze(1)).then_inc(s["r_sev"], 1)


def choose(nc, ident, iota, scores, picks):
    NH2 = H * TOPK
    with ExitStack() as ctx:
        def sb(name, shape, dt=F32):
            return ctx.enter_context(nc.sbuf_tensor(name, shape, dt))

        st = sb("c_st", [P, HP, NK])
        val = sb("c_val", [P, HP, TOPK])
        idx = sb("c_idx", [P, HP, TOPK], U32)
        idf = sb("c_idf", [P, HP, TOPK])
        best = sb("c_best", [P, H, TOPK])
        at = sb("c_at", [P, H, TOPK], U32)
        ab = sb("c_ab", [P, 2, NH2], U32)
        abf = sb("c_abf", [P, 2, NH2])
        eq = sb("c_eq", [P, NH2, TOPK])
        out = sb("c_out", [P, 3, NH2])
        tot = sb("c_tot", [P, H])
        inv = sb("c_inv", [P, H])
        pad = sb("c_pad", [P, 2])
        turn = ctx.enter_context(nc.psum_tensor("c_turn", [P, 512], F32))
        s = with_sems(nc, ctx, """c_st c_m1 c_i1 c_r c_m2 c_i2 c_idf c_cand c_fm1 c_fi1 c_fr c_fm2 c_fi2 c_ab c_abf
            c_eq c_pk c_sum c_sub c_exp c_tot c_inv c_gate c_tr c_ev c_pad""")
        block = ctx.enter_context(nc.Block())
        cand = st[:].rearrange("p s n -> p (s n)").rearrange("p (h c) -> p h c", h=H)

        @block.scalar
        def _(act):
            with act.Fori(0, TILES) as t:
                act.wait_ge(s["c_fi2"], t)
                act.activation(st[:].unsqueeze(1), scores[:, bass.ds(t, 1), :, :], ACT.Copy).then_inc(s["c_st"], 1)
                act.wait_ge(s["c_sub"], t + 1)
                act.activation(out[:, 0, :], out[:, 0, :], ACT.Exp).then_inc(s["c_exp"], 1)
                act.wait_ge(s["c_tr"], t + 1)
                act.activation(picks[:, :, bass.ds(t * P, P)], turn[:, 0:3 * P].rearrange("p (k t) -> p k t", k=3),
                               ACT.Copy).then_inc(s["c_ev"], 1)

        @block.tensor
        def _(pe):
            with pe.Fori(0, TILES) as t:
                pe.wait_ge(s["c_gate"], t + 1)
                pe.wait_ge(s["c_sum"], 2 * t + 2)
                pe.wait_ge(s["c_ev"], t)
                for k in range(3):
                    mm = pe.transpose(turn[:, k * P:(k + 1) * P], out[:, k, :], ident[:])
                mm.then_inc(s["c_tr"], 1)

        @block.vector
        def _(dve):
            dve.memset(pad[:], 0.0).then_inc(s["c_pad"], 1)
            dve.wait_ge(s["c_pad"], 1)

            def settled(name, t):
                dve.wait_ge(s[name], t + 1)
                dve.tensor_copy(pad[:, 1:2], pad[:, 0:1])

            def top16(src, n, v, i, t, sems):
                m1, i1, r, m2, i2 = sems
                for q in range(n):
                    op = dve.max(v[:, q, 0:8], src[:, q, :])
                op.then_inc(s[m1], 1)
                settled(m1, t)
                for q in range(n):
                    op = dve.max_index(i[:, q, 0:8], v[:, q, 0:8], src[:, q, :])
                op.then_inc(s[i1], 1)
                settled(i1, t)
                for q in range(n):
                    op = dve.match_replace(out=src[:, q, :], in_to_replace=v[:, q, 0:8], in_values=src[:, q, :],
                                           imm_value=NEG)
                op.then_inc(s[r], 1)
                settled(r, t)
                for q in range(n):
                    op = dve.max(v[:, q, 8:16], src[:, q, :])
                op.then_inc(s[m2], 1)
                settled(m2, t)
                for q in range(n):
                    op = dve.max_index(i[:, q, 8:16], v[:, q, 8:16], src[:, q, :])
                op.then_inc(s[i2], 1)

            with dve.Fori(0, TILES) as t:
                settled("c_st", t)
                top16(st, HP, val, idx, t, ("c_m1", "c_i1", "c_r", "c_m2", "c_i2"))
                dve.wait_ge(s["c_i2"], t + 1)
                dve.tensor_copy(idf[:], idx[:]).then_inc(s["c_idf"], 1)
                vv = val[:].rearrange("p (h k) i -> p h k i", k=2)
                dve.tensor_tensor(cand.rearrange("p h (i j) -> p h i j", j=TOPK),
                                  vv[:, :, 0, :].unsqueeze(3).to_broadcast((P, H, TOPK, TOPK)),
                                  vv[:, :, 1, :].unsqueeze(2).to_broadcast((P, H, TOPK, TOPK)),
                                  ALU.add).then_inc(s["c_cand"], 1)
                settled("c_cand", t)
                top16(cand, H, best, at, t, ("c_fm1", "c_fi1", "c_fr", "c_fm2", "c_fi2"))
                dve.wait_ge(s["c_fi2"], t + 1)
                flat = at[:].rearrange("p h k -> p (h k)")
                dve.tensor_scalar(ab[:, 0, :], flat, 4, None, ALU.logical_shift_right).then_inc(s["c_ab"], 1)
                dve.tensor_scalar(ab[:, 1, :], flat, 15, None, ALU.bitwise_and).then_inc(s["c_ab"], 1)
                dve.wait_ge(s["c_ab"], 2 * t + 2)
                dve.tensor_copy(abf[:], ab[:]).then_inc(s["c_abf"], 1)
                dve.wait_ge(s["c_tr"], t)
                dve.tensor_tensor(out[:, 0, :].rearrange("p (h k) -> p h k", h=H), best[:],
                                  best[:, :, 0:1].to_broadcast((P, H, TOPK)), ALU.subtract).then_inc(s["c_sub"], 1)
                dve.wait_ge(s["c_abf"], t + 1)
                dve.wait_ge(s["c_idf"], t + 1)
                ii = idf[:].rearrange("p (h k) i -> p h k i", k=2)
                for k in range(2):
                    dve.tensor_tensor(eq[:], abf[:, k, :].unsqueeze(2).to_broadcast((P, NH2, TOPK)),
                                      iota[:, 0:TOPK].unsqueeze(1).to_broadcast((P, NH2, TOPK)),
                                      ALU.is_equal).then_inc(s["c_eq"], 1)
                    dve.wait_ge(s["c_eq"], 2 * t + k + 1)
                    e4 = eq[:].rearrange("p (h k) i -> p h k i", h=H)
                    dve.tensor_tensor(e4, e4, ii[:, :, k, :].unsqueeze(2).to_broadcast((P, H, TOPK, TOPK)),
                                      ALU.mult).then_inc(s["c_pk"], 1)
                    dve.wait_ge(s["c_pk"], 2 * t + k + 1)
                    dve.tensor_reduce(out[:, 1 + k, :], eq[:], AX, ALU.add).then_inc(s["c_sum"], 1)
                    if k == 0:
                        dve.wait_ge(s["c_sum"], 2 * t + 1)
                dve.wait_ge(s["c_exp"], t + 1)
                g3 = out[:, 0, :].rearrange("p (h k) -> p h k", h=H)
                dve.tensor_reduce(tot[:], g3, AX, ALU.add).then_inc(s["c_tot"], 1)
                dve.wait_ge(s["c_tot"], t + 1)
                dve.reciprocal(inv[:], tot[:]).then_inc(s["c_inv"], 1)
                dve.wait_ge(s["c_inv"], t + 1)
                dve.tensor_tensor(g3, g3, inv[:].unsqueeze(2).to_broadcast((P, H, TOPK)),
                                  ALU.mult).then_inc(s["c_gate"], 1)


def gate_matrix(nc, a, picks):
    GRP = 4
    NG = GT // GRP
    RING = 4
    BODY = 2 * NG
    assert BODY % RING == 0
    on_act = [q for q in range(BODY) if q % 3 == 0]
    on_pool = [q for q in range(BODY) if q % 3]
    with ExitStack() as ctx:
        def sb(name, shape, dt=F32):
            return ctx.enter_context(nc.sbuf_tensor(name, shape, dt))

        iota = sb("g_iota", [P, P])
        hot = [sb(f"g_hot{r}", [P, 2, GRP, NK]) for r in range(RING)]
        stage = [sb(f"g_stage{e}", [P, NK, GT]) for e in range(2)]
        acc = [ctx.enter_context(nc.psum_tensor(f"g_acc{r}", [P, 512], F32)) for r in range(RING)]
        s = with_sems(nc, ctx, "g_in g_hot g_act g_pool g_mm g_ev g_st0 g_st1")
        stored = [s["g_st0"], s["g_st1"]]
        block = ctx.enter_context(nc.Block())

        @block.sync
        def _(sp):
            sp.dma_start(iota[:], a["iota"]).then_inc(s["g_in"], 16)
            with sp.Fori(0, GB // 2) as m:
                for e in range(2):
                    sp.wait_ge(s["g_ev"], (2 * m + e + 1) * NG)
                    sp.dma_start(a["gates_d"][:, bass.ds(2 * m + e, 1)].rearrange("p o i t -> p (o i t)"),
                                 stage[e][:].rearrange("p i t -> p (i t)")).then_inc(stored[e], 16)
            for e in range(2):
                sp.wait_ge(stored[e], 16 * (GB // 2))

        @block.vector
        def _(dve):
            dve.wait_ge(s["g_in"], 16)
            with dve.Fori(0, GB // 2) as m:
                for q in range(BODY):
                    dve.wait_ge(s["g_mm"], BODY * m + max(q - RING + 1, 0))
                    dve.tensor_tensor(hot[q % RING][:],
                                      iota[:].unsqueeze(1).unsqueeze(1).to_broadcast((P, 2, GRP, NK)),
                                      picks[:, 1:3, bass.ds(2 * GT * m + GRP * q, GRP)].unsqueeze(3)
                                      .to_broadcast((P, 2, GRP, NK)), ALU.is_equal).then_inc(s["g_hot"], 1)

        @block.gpsimd
        def _(pool):
            with pool.Fori(0, GB // 2) as m:
                for q in on_pool:
                    two = hot[q % RING][:, 1]
                    pool.wait_ge(s["g_hot"], BODY * m + q + 1)
                    pool.tensor_tensor(two, two, picks[:, 0, bass.ds(2 * GT * m + GRP * q, GRP)].unsqueeze(2)
                                       .to_broadcast((P, GRP, NK)), ALU.mult).then_inc(s["g_pool"], 1)

        @block.tensor
        def _(pe):
            with pe.Fori(0, GB // 2) as m:
                for q in range(BODY):
                    if q in on_act:
                        pe.wait_ge(s["g_act"], len(on_act) * m + on_act.index(q) + 1)
                    else:
                        pe.wait_ge(s["g_pool"], len(on_pool) * m + on_pool.index(q) + 1)
                    pe.wait_ge(s["g_hot"], BODY * m + q + 1)
                    pe.wait_ge(s["g_ev"], BODY * m + max(q - RING + 1, 0))
                    for j in range(GRP):
                        mm = pe.matmul(acc[q % RING][:, j * NK:(j + 1) * NK], hot[q % RING][:, 0, j, :],
                                       hot[q % RING][:, 1, j, :], start=True, stop=True)
                    mm.then_inc(s["g_mm"], 1)

        @block.scalar
        def _(act):
            LAG = 2
            with act.Fori(0, GB // 2) as m:
                for q in range(BODY + LAG):
                    if q in on_act:
                        act.wait_ge(s["g_hot"], BODY * m + q + 1)
                        for j in range(GRP):
                            row = hot[q % RING][:, 1, j, :]
                            op = act.activation(row, row, ACT.Copy,
                                                scale=picks[:, 0, bass.ds(2 * GT * m + GRP * q + j, 1)])
                        op.then_inc(s["g_act"], 1)
                    if q < LAG:
                        continue
                    e, g = divmod(q - LAG, NG)
                    if g == 0:
                        act.wait_ge(stored[e], 16 * m)
                    act.wait_ge(s["g_mm"], BODY * m + q - LAG + 1)
                    act.activation(stage[e][:, :, GRP * g:GRP * (g + 1)],
                                   acc[(q - LAG) % RING][:, :].rearrange("p (t i) -> p i t", t=GRP),
                                   ACT.Copy).then_inc(s["g_ev"], 1)


def experts(nc, a, h2, y):
    h2h, h2l = h2
    LAST = NK - 1
    with ExitStack() as ctx:
        def sb(name, shape, dt=F32):
            return ctx.enter_context(nc.sbuf_tensor(name, shape, dt))

        u = [sb(f"e_u{r}", [P, KD, P]) for r in range(2)]
        uh = [sb(f"e_uh{r}", [P, KD, P], F32R) for r in range(2)]
        ul = [sb(f"e_ul{r}", [P, KD, P], F32R) for r in range(2)]
        v = sb("e_v", [P, 2, D])
        vh = sb("e_vh", [P, 2, D], F32R)
        vl = sb("e_vl", [P, 2, D], F32R)
        gate = [sb(f"e_gate{r}", [P, GB, 2, GT]) for r in range(2)]
        gelu = [sb(f"e_gelu{r}", [P, TB]) for r in range(2)]
        wf = [sb(f"e_wf{r}", [P, TB]) for r in range(2)]
        wh = [sb(f"e_wh{r}", [P, NT], F32R) for r in range(4)]
        wl = [sb(f"e_wl{r}", [P, NT], F32R) for r in range(4)]
        a_b = [ctx.enter_context(nc.psum_tensor(f"e_a{r}", [P, 512], F32)) for r in range(2)]
        y_b = [ctx.enter_context(nc.psum_tensor(f"e_y{r}", [P, 512], F32)) for r in range(4)]
        s = with_sems(nc, ctx, """e_uin0 e_uin1 e_vin e_gin0 e_gin1 e_uh e_ul e_vh e_vl e_a e_gelu e_wf e_wh e_wl
            e_y e_yadd""")
        u_in = [s["e_uin0"], s["e_uin1"]]
        g_in = [s["e_gin0"], s["e_gin1"]]
        block = ctx.enter_context(nc.Block())
        YB = 3 * KD
        GB3 = GB // 3

        @block.sync
        def _(sp):
            def load_u(j, r):
                after(sp, s["e_ul"], j - 1)
                sp.dma_start(u[r][:], a["uT"][bass.ds(j, 1)].rearrange("o p k c -> (o p) k c")).then_inc(u_in[r], 16)

            def load_v(p):
                after(sp, s["e_vl"], p)
                sp.dma_start(v[:], a["v"][:, bass.ds(2 * p, 2), :]).then_inc(s["e_vin"], 16)

            def load_gate(p, r):
                after(sp, s["e_wf"], 6 * (p - 1))
                sp.dma_start(gate[r][:], a["gates_d"][:, :, bass.ds(2 * p, 2), :]).then_inc(g_in[r], 16)

            load_u(0, 0)
            load_gate(0, 0)
            load_u(1, 1)
            load_v(0)

            def body(i, last):
                load_u(4 * i + 2, 0)
                load_gate(2 * i + 1, 1)
                load_u(4 * i + 3, 1)
                load_v(2 * i + 1)
                if not last:
                    load_u(4 * i + 4, 0)
                    load_gate(2 * i + 2, 0)
                    load_u(4 * i + 5, 1)
                    load_v(2 * i + 2)
            body(0, False)
            with sp.Fori(1, NK // 4 - 1) as i:
                body(i, False)
            body(NK // 4 - 1, True)

        @block.tensor
        def _(pe):
            def make_a(j, q, r):
                pe.wait_ge(s["e_uh"], j + 1)
                pe.wait_ge(s["e_ul"], j + 1)
                for b in range(3):
                    after(pe, s["e_gelu"], 3 * j + b - 1)
                    o = a_b[(r + b) % 2][:, 0:TB]
                    cols = slice(b * TB, (b + 1) * TB)
                    for k in range(KD):
                        pe.matmul(o, uh[q][:, k, :], h2h[:, k, cols], start=k == 0, stop=False)
                        pe.matmul(o, uh[q][:, k, :], h2l[:, k, cols], start=False, stop=False)
                        mm = pe.matmul(o, ul[q][:, k, :], h2h[:, k, cols], start=False, stop=k == KD - 1)
                    mm.then_inc(s["e_a"], 1)

            def add_values(p, slots):
                pe.wait_ge(s["e_vh"], p + 1)
                pe.wait_ge(s["e_vl"], p + 1)
                pe.wait_ge(s["e_wl"], 6 * p + 6)
                n = 0
                for k in range(KD):
                    for b in range(3):
                        after(pe, s["e_yadd"], YB * p + max(n - 3, 0))
                        cols = slice(b * TB, (b + 1) * TB)
                        o = y_b[n % 4][:, 0:TB]
                        for c, r in enumerate(slots):
                            h, l = vh[:, c, k * P:(k + 1) * P], vl[:, c, k * P:(k + 1) * P]
                            pe.matmul(o, h, wh[r][:, cols], start=c == 0, stop=False)
                            pe.matmul(o, h, wl[r][:, cols], start=False, stop=False)
                            mm = pe.matmul(o, l, wh[r][:, cols], start=False, stop=c == 1)
                        mm.then_inc(s["e_y"], 1)
                        n += 1

            def body(i, last):
                make_a(4 * i + 1, 1, 1)
                make_a(4 * i + 2, 0, 0)
                add_values(2 * i, (0, 1))
                make_a(4 * i + 3, 1, 1)
                if not last:
                    make_a(4 * i + 4, 0, 0)
                add_values(2 * i + 1, (2, 3))
            make_a(0, 0, 0)
            with pe.Fori(0, NK // 4 - 1) as i:
                body(i, False)
            body(NK // 4 - 1, True)

        @block.scalar
        def _(act):
            def split_u(j, r):
                act.wait_ge(u_in[r], 16 * (j // 2 + 1) if isinstance(j, int) else 8 * (j - r) + 16)
                after(act, s["e_a"], 3 * (j - 1))
                act.activation(uh[r][:], u[r][:], ACT.Copy).then_inc(s["e_uh"], 1)

            def split_v(p):
                act.wait_ge(s["e_vin"], 16 * p + 16)
                after(act, s["e_y"], YB * p)
                act.activation(vh[:], v[:], ACT.Copy).then_inc(s["e_vh"], 1)

            def weigh(j, r, slot):
                for b in range(3):
                    act.wait_ge(s["e_a"], 3 * j + b + 1)
                    after(act, s["e_wf"], 3 * j + b - 1)
                    act.activation(gelu[(r + b) % 2][:], a_b[(r + b) % 2][:, 0:TB], ACT.Gelu).then_inc(s["e_gelu"], 1)
                    act.wait_ge(s["e_wf"], 3 * j + b + 1)
                    act.activation(wh[slot][:, b * TB:(b + 1) * TB], wf[(r + b) % 2][:], ACT.Copy
                                   ).then_inc(s["e_wh"], 1)

            def body(i, last):
                split_u(4 * i + 2, 0)
                weigh(4 * i + 1, 1, 1)
                split_v(2 * i)
                split_u(4 * i + 3, 1)
                weigh(4 * i + 2, 0, 2)
                if not last:
                    split_u(4 * i + 4, 0)
                weigh(4 * i + 3, 1, 3)
                split_v(2 * i + 1)
                if not last:
                    split_u(4 * i + 5, 1)
                    weigh(4 * i + 4, 0, 0)
            split_u(0, 0)
            split_u(1, 1)
            weigh(0, 0, 0)
            body(0, False)
            with act.Fori(1, NK // 4 - 1) as i:
                body(i, False)
            body(NK // 4 - 1, True)

        @block.vector
        def _(dve):
            def split_u(j, r):
                after(dve, s["e_a"], 3 * (j - 1))
                dve.wait_ge(s["e_uh"], j + 1)
                dve.tensor_tensor(ul[r][:], u[r][:], uh[r][:].bitcast(F32), ALU.subtract).then_inc(s["e_ul"], 1)

            def split_v(p):
                after(dve, s["e_y"], YB * p)
                dve.wait_ge(s["e_vh"], p + 1)
                dve.tensor_tensor(vl[:], v[:], vh[:].bitcast(F32), ALU.subtract).then_inc(s["e_vl"], 1)

            def weigh(j, r, slot, g, gcount, free):
                dve.wait_ge(g_in[g], gcount)
                after(dve, s["e_y"], free)
                for b in range(3):
                    dve.wait_ge(s["e_gelu"], 3 * j + b + 1)
                    after(dve, s["e_wh"], 3 * j + b - 1)
                    w3 = lambda x: x.rearrange("p (b t) -> p b t", t=GT)
                    dve.tensor_tensor(w3(wf[(r + b) % 2][:]), w3(gelu[(r + b) % 2][:]),
                                      gate[g][:, GB3 * b:GB3 * (b + 1), slot % 2, :], ALU.mult).then_inc(s["e_wf"], 1)
                    dve.wait_ge(s["e_wh"], 3 * j + b + 1)
                    cols = slice(b * TB, (b + 1) * TB)
                    dve.tensor_tensor(wl[slot][:, cols], wf[(r + b) % 2][:], wh[slot][:, cols].bitcast(F32),
                                      ALU.subtract).then_inc(s["e_wl"], 1)

            def add(p, first):
                n = 0
                for k in range(KD):
                    for b in range(3):
                        dve.wait_ge(s["e_y"], YB * p + n + 1)
                        after(dve, s["e_yadd"], YB * p)
                        cols = slice(b * TB, (b + 1) * TB)
                        if first:
                            dve.tensor_copy(y[:, k, cols], y_b[n % 4][:, 0:TB]).then_inc(s["e_yadd"], 1)
                        else:
                            dve.tensor_tensor(y[:, k, cols], y_b[n % 4][:, 0:TB], y[:, k, cols],
                                              ALU.add).then_inc(s["e_yadd"], 1)
                        n += 1

            def body(i, first, last):
                split_u(4 * i + 2, 0)
                weigh(4 * i + 1, 1, 1, 0, 16 * i + 16, YB * 2 * i)
                split_v(2 * i)
                split_u(4 * i + 3, 1)
                weigh(4 * i + 2, 0, 2, 1, 16 * i + 16, YB * 2 * i)
                if not last:
                    split_u(4 * i + 4, 0)
                add(2 * i, first)
                weigh(4 * i + 3, 1, 3, 1, 16 * i + 16, YB * 2 * i)
                split_v(2 * i + 1)
                if not last:
                    split_u(4 * i + 5, 1)
                    weigh(4 * i + 4, 0, 0, 0, 16 * i + 32, YB * (2 * i + 1))
                add(2 * i + 1, False)
            split_u(0, 0)
            split_u(1, 1)
            weigh(0, 0, 0, 0, 16, 0)
            body(0, True, False)
            with dve.Fori(1, NK // 4 - 1) as i:
                body(i, False, False)
            body(NK // 4 - 1, False, True)


def finish(nc, a, y):
    with ExitStack() as ctx:
        ident = ctx.enter_context(nc.sbuf_tensor("z_ident", [P, P], F32))
        x1 = [ctx.enter_context(nc.sbuf_tensor(f"z_x1_{e}", [P, D], F32)) for e in range(2)]
        bank = [ctx.enter_context(nc.psum_tensor(f"z_b{e}", [P, D], F32)) for e in range(2)]
        s = with_sems(nc, ctx, "z_id z_in0 z_in1 z_tr z_add z_st0 z_st1")
        x_in = [s["z_in0"], s["z_in1"]]
        stored = [s["z_st0"], s["z_st1"]]
        rows = [P] * PT_TILES + [NS]
        block = ctx.enter_context(nc.Block())

        @block.sync
        def _(sp):
            sp.dma_start(ident[:], a["ident"]).then_inc(s["z_id"], 16)
            for t, n in enumerate(rows):
                if t >= 2:
                    sp.wait_ge(stored[t % 2], 16 * (t // 2))
                sp.dma_start(x1[t % 2][:], a["x1_d"][t * P:(t + 1) * P, :]).then_inc(x_in[t % 2], 16)
                if t >= 1:
                    sp.wait_ge(s["z_add"], 2 * t)
                    sp.dma_start(a["y_all"][(t - 1) * P:t * P, :], x1[(t - 1) % 2][:]).then_inc(stored[(t - 1) % 2], 16)
            sp.wait_ge(s["z_add"], 2 * TILES)
            sp.dma_start(a["y_all"][SEQ:NT, :], x1[PT_TILES % 2][0:NS, :]).then_inc(stored[PT_TILES % 2], 16)
            for e in range(2):
                sp.wait_ge(stored[e], 16 * ((TILES + 1 - e) // 2))

        @block.tensor
        def _(pe):
            pe.wait_ge(s["z_id"], 16)
            for t, n in enumerate(rows):
                if t >= 2:
                    pe.wait_ge(s["z_add"], 2 * (t - 1))
                for k in range(KD):
                    mm = pe.transpose(bank[t % 2][0:n, k * P:(k + 1) * P], y[:, k, t * P:t * P + n], ident[:])
                mm.then_inc(s["z_tr"], 1)

        @block.vector
        def _(dve):
            for t, n in enumerate(rows):
                dve.wait_ge(s["z_tr"], t + 1)
                dve.wait_ge(x_in[t % 2], 16 * (t // 2 + 1))
                for c in range(2):
                    cols = slice(c * 512, (c + 1) * 512)
                    dve.tensor_tensor(x1[t % 2][0:n, cols], bank[t % 2][0:n, cols], x1[t % 2][0:n, cols],
                                      ALU.add).then_inc(s["z_add"], 1)


def build_step(nc, a):
    a["pin_d"] = nc.dram_tensor("pin_d", [NPAD, PW], F32).ap()
    a["mixT_d"] = nc.dram_tensor("mixT_d", [P, G4, NPAD], F32).ap()
    a["x1_d"] = nc.dram_tensor("x1_d", [NPAD, D], F32).ap()
    a["h2T_d"] = nc.dram_tensor("h2T_d", [P, KD, NT], F32).ap()
    a["gates_d"] = nc.dram_tensor("gates_d", [P, GB, NK, GT], F32).ap()
    with nc.sbuf_tensor("qkT", [P, 2 * H, NPAD], F32) as qkT:
        with nc.sbuf_tensor("vall", [P, TILES, H * VD], F32) as vall:
            mixer_front(nc, a, qkT, vall)
            prompt_attention(nc, a, qkT, vall)
        sample_attention(nc, a, qkT)
    mixer_out(nc, a)
    with nc.sbuf_tensor("h2h", [P, KD, NT], F32R) as h2h, nc.sbuf_tensor("h2l", [P, KD, NT], F32R) as h2l:
        with nc.sbuf_tensor("picks", [P, 3, NPAD], F32) as picks:
            router(nc, a, (h2h, h2l), picks)
            gate_matrix(nc, a, picks)
        with nc.sbuf_tensor("y", [P, KD, NT], F32) as y:
            experts(nc, a, (h2h, h2l), y)
            finish(nc, a, y)




def shape_constants():
    f = np.float32
    pos = np.zeros(NPAD, f)
    pos[:SEQ] = np.arange(SEQ)
    pos[SEQ:NT] = PAST + np.tile(np.arange(DEC_S), DEC_B)
    inv = (np.float32(10000.0) ** (-np.arange(HALF, dtype=f) / f(HALF))).astype(f)
    ang = (pos[:, None] * inv[None, :]).astype(f)
    cos, sin = np.cos(ang), np.sin(ang)
    tiles = lambda m: np.ascontiguousarray(m.reshape(TILES, P, ROPE).transpose(1, 0, 2).astype(f))
    out = {
        "ident": np.eye(P, dtype=f),
        "rope_c": tiles(np.concatenate([cos, cos], 1)),
        "rope_s": tiles(np.concatenate([-sin, sin], 1)),
        "causal": np.where(np.arange(P)[None, :] <= np.arange(P)[:, None], f(0), f(NEG)),
        "iota": np.tile(np.arange(P, dtype=f), (P, 1)),
    }
    band = np.zeros((P, 5, G4, P), f)
    t = np.arange(P)
    for g, w in enumerate(WINDOWS):
        for kind, at, count in ((0, 0, np.minimum(w, t + 1)), (1, 0, np.full(P, w)), (2, -P, np.full(P, w))):
            src = t[:, None] + at
            inside = (src <= t[None, :]) & (src > t[None, :] - w)
            band[:, kind, g, :] = np.where(inside, f(1) / count[None, :].astype(f), f(0)) - (src == t[None, :])
        for b in range(DEC_B):
            for o in range(DEC_S):
                for r in range(DEC_S):
                    band[b * DEC_S + r, 3, g, b * DEC_S + o] = (r <= o and r > o - w) / f(w) - (r == o)
                for r in range(PSTATE):
                    band[b * PSTATE + r, 4, g, b * DEC_S + o] = (r - PSTATE > o - w) / f(w)
    out["band"] = band
    ok = np.arange(DEC_S)[:, None] <= np.arange(DEC_S)[None, :]
    out["newmask"] = np.ascontiguousarray(np.broadcast_to(np.where(ok, f(0), f(NEG))[:, None, :], (DEC_S, H, DEC_S)))
    return out


def layouts(i):
    f = np.float32
    c = np.ascontiguousarray
    x = np.zeros((NPAD, D), f)
    x[:SEQ], x[SEQ:NT] = i["x_prompt"][0], i["x_sample"].reshape(NS, D)
    rows = lambda w, k: c(w.reshape(k, P, -1).transpose(1, 0, 2))
    lat, kr = i["cache_kv_latent"], i["cache_k_rope"]
    n_phys = lat.shape[0]
    page = np.zeros((n_phys, P, 2 * KVL + ROPE), f)
    page[:, :, 0:KVL] = lat.transpose(0, 2, 1).reshape(n_phys, CT, P, P).transpose(0, 2, 1, 3).reshape(n_phys, P, KVL)
    page[:, :, KVL:2 * KVL] = lat
    page[:, :, 2 * KVL:] = kr
    state = np.zeros((P, PW), f)
    state[:DEC_B * PSTATE] = i["state_pool"].reshape(DEC_B * PSTATE, PW)
    u = i["peer_u"].reshape(NK, NK, KD, P)
    v = i["peer_v"].reshape(NK, NK, D)
    return {
        "x": x,
        "xT": c(x.T.reshape(KD, P, NPAD).transpose(1, 0, 2)),
        "w_in": rows(i["w_in"], KD), "w_q_up": rows(i["w_q_up"], QT),
        "w_uk": rows(i["w_uk"].reshape(KVL, -1), CT), "w_uv": rows(i["w_uv"].reshape(KVL, -1), CT),
        "w_ukT": c(i["w_uk"].transpose(2, 1, 0)),
        "g_attn": c(i["g_attn"].reshape(KD, P).T), "g_q_lat": c(i["g_q_lat"].reshape(QT, P).T),
        "g_kv_lat": i["g_kv_lat"][None], "g_q_nope": i["g_q_nope"][None], "g_q_rope": i["g_q_rope"][None],
        "g_k_nope": i["g_k_nope"][None], "g_k_rope": i["g_k_rope"][None],
        "g_k_col": c(np.concatenate([i["g_k_nope"], i["g_k_rope"], i["g_k_rope"]])[:, None]),
        "page": page, "page_krT": c(kr.transpose(0, 2, 1)),
        "page_table": i["page_table"].astype(np.int32, copy=False),
        "state": state, "state_pool": i["state_pool"],
        "w_pool": c(i["w_pool"].transpose(1, 0, 2)), "pool_scale": c(i["pool_scale"].reshape(G4, P).T),
        "w_o": rows(i["w_o"], KD), "g_ffn": c(i["g_ffn"].reshape(KD, P).T),
        "w_pq": c(i["w_pq"].reshape(KD, P, HP, P).transpose(2, 1, 0, 3)),
        "keysT": c(i["peer_keys"].reshape(HP, NK, P).transpose(2, 0, 1)),
        "uT": c(u.transpose(1, 3, 2, 0)),
        "v": v,
    }


OUTS = {
    "y_all": [NT, D], "kv_all": [NPAD, KVL], "kr_all": [NPAD, ROPE],
    "pool_prompt": [PSTATE, PW], "pool_sample": [DEC_B, PSTATE, PW],
}


def kernel(**inputs):
    import concourse.bacc as bacc
    from concourse.bass_utils import run_bass_kernel_spmd

    arrays = {**layouts({k: np.asarray(v) for k, v in inputs.items()}), **shape_constants()}
    nc = bacc.Bacc("TRN2", target_bir_lowering=False, num_devices=1)
    a = {n: nc.dram_tensor(n, list(v.shape), mybir.dt.from_np(v.dtype), kind="ExternalInput").ap()
         for n, v in arrays.items()}
    for n, shape in OUTS.items():
        a[n] = nc.dram_tensor(n, shape, F32, kind="ExternalOutput").ap()
    build_step(nc, a)
    r = run_bass_kernel_spmd(nc, [arrays], core_ids=[0]).results[0]
    return (r["y_all"][None, :SEQ], r["y_all"][SEQ:].reshape(DEC_B, DEC_S, D),
            r["kv_all"][None, :SEQ], r["kr_all"][None, :SEQ], r["pool_prompt"][None],
            r["kv_all"][SEQ:NT].reshape(DEC_B, DEC_S, KVL), r["kr_all"][SEQ:NT].reshape(DEC_B, DEC_S, ROPE),
            r["pool_sample"])
```

```python
from contextlib import ExitStack

import numpy as np

import concourse.bass as bass
from concourse import mybir

F32 = mybir.dt.float32
F32R = mybir.dt.float32r
U32 = mybir.dt.uint32
I32 = mybir.dt.int32
ALU = mybir.AluOpType
ACT = mybir.ActivationFunctionType
AX = mybir.AxisListType.X

P = 128
D = 1024
KD = D // P
SEQ = 1024
DEC_B, DEC_S = 8, 4
NS = DEC_B * DEC_S
NT = SEQ + NS
TILES = SEQ // P + 1
PT_TILES = SEQ // P
NPAD = TILES * P
PAST = 2048
PAGES = PAST // P
H = 8
NOPE, ROPE, VD = 64, 32, 64
HD = NOPE + ROPE
HALF = ROPE // 2
QL, KVL = 384, 256
QT, CT = QL // P, KVL // P
PW = 512
G4 = 4
WINDOWS = (2, 4, 8, 16)
PSTATE = 15
IN_W = QL + KVL + ROPE + PW
EPS = 1e-6
SM = HD ** -0.5
NK = 128
HP = 16
TOPK = 16
TB = NT // 3
GT = 88
GB = NT // GT
NEG = -3.0e38


def with_sems(nc, ctx, names):
    sems = {n: nc.alloc_semaphore(n) for n in names.split()}

    def release():
        nc.clear_and_free_semaphores(list(sems.values()))
        nc.all_engine_barrier()
    ctx.callback(release)
    return sems


def after(eng, sem, value):
    if isinstance(value, int) and value <= 0:
        return
    eng.wait_ge(sem, value)


def mixer_front(nc, a, qkT, vall, kept):
    with ExitStack() as ctx:
        def sb(name, shape, dt=F32):
            return ctx.enter_context(nc.sbuf_tensor(name, shape, dt))

        w_in = sb("f_w_in", [P, KD, IN_W])
        w_q = sb("f_w_q", [P, QT, H * HD])
        w_uk, w_uv, ident = kept["w_uk"], kept["w_uv"], kept["ident"]
        g_attn = sb("f_g_attn", [P, KD])
        g_ql = sb("f_g_ql", [P, QT])
        g_kv = sb("f_g_kv", [P, KVL])
        g_qk = sb("f_g_qk", [P, 2, HD])
        rope_c = sb("f_rope_c", [P, TILES, ROPE])
        rope_s = sb("f_rope_s", [P, TILES, ROPE])
        eps = sb("f_eps", [P, 1])
        x_t = sb("f_x", [P, D])
        xT = sb("f_xT", [P, KD, P])
        junk = sb("f_junk", [P, 2 * H * HD])
        zq = sb("f_zq", [P, QL])
        zck = sb("f_zck", [P, KVL + ROPE])
        pin = sb("f_pin", [P, PW])
        c_t = sb("f_c", [P, KVL])
        kr = sb("f_kr", [P, ROPE])
        r_a = sb("f_ra", [P, H, ROPE])
        r_b = sb("f_rb", [P, H, ROPE])
        qlT = sb("f_qlT", [P, QT, P])
        cT = sb("f_cT", [P, CT, P])
        qk = sb("f_qk", [P, 2 * H, HD])
        ss = sb("f_ss", [P, 1])
        rstd = sb("f_rstd", [P, 1])
        ss2 = sb("f_ss2", [P, 2])
        rstd2 = sb("f_rstd2", [P, 2])
        ssh = sb("f_ssh", [P, 2 * H])
        rstdh = sb("f_rstdh", [P, 2 * H])
        banks = [ctx.enter_context(nc.psum_tensor(f"f_b{i}", [P, 512], F32)) for i in range(8)]

        s = with_sems(nc, ctx, """f_wts f_gain f_win0 f_win1 f_win2 f_win3 f_kept f_x_in f_consts f_w_scaled f_z f_sqx f_std f_rstd f_zq f_zck f_pin
            f_ms f_std2 f_rstd2 f_qlt f_qlT f_q f_qev f_c f_ct f_cT f_kv f_kev f_vev f_ra f_rb f_kr f_kpe
            f_sqh f_ssh f_stdh f_rstdh f_n1 f_n2 f_qra f_qrb f_rot f_tr0 f_tr1 f_ev0 f_ev1 f_out""")
        block = ctx.enter_context(nc.Block())

        CHUNKS = 4
        chunk_in = [s[f"f_win{c}"] for c in range(CHUNKS)]

        def chunk(c):
            return slice(c * KD // CHUNKS, (c + 1) * KD // CHUNKS)

        def tiles(eng, project, rest):
            project(0)
            with eng.Fori(0, TILES - 1) as t:
                rest(t, lambda: project(t + 1))
            rest(TILES - 1, lambda: None)

        @block.sync
        def _(sp):
            sp.dma_start(g_attn[:], a["g_attn"]).then_inc(s["f_gain"], 16)

            def load(t):
                after(sp, s["f_z"], t)
                after(sp, s["f_sqx"], t)
                sp.dma_start(x_t[:], a["x"][bass.ds(t * P, P), :]).then_inc(s["f_x_in"], 16)
                sp.dma_start(xT[:], a["xT"][:, :, bass.ds(t * P, P)]).then_inc(s["f_x_in"], 16)
            for c in range(CHUNKS):
                sp.dma_start(w_in[:, chunk(c), :], a["w_in"][:, chunk(c), :]).then_inc(chunk_in[c], 16)
                if c == 0:
                    load(0)
            for dst, src in ((w_q, a["w_q_up"]), (g_ql, a["g_q_lat"]), (ident, a["ident"]),
                             (w_uk, a["w_uk"]), (w_uv, a["w_uv"]),
                             (rope_c, a["rope_c"]), (rope_s, a["rope_s"]),
                             (g_kv, a["g_kv_lat"].to_broadcast((P, KVL)))):
                sp.dma_start(dst[:], src).then_inc(s["f_wts"], 16)
            for i, n in enumerate(("q", "k")):
                sp.dma_start(g_qk[:, i, 0:NOPE], a[f"g_{n}_nope"].to_broadcast((P, NOPE))).then_inc(s["f_wts"], 16)
                for r in range(2):
                    sp.dma_start(g_qk[:, i, NOPE + r * HALF:NOPE + (r + 1) * HALF],
                                 a[f"g_{n}_rope"].to_broadcast((P, HALF))).then_inc(s["f_wts"], 16)

            sp.dma_start(kept["w_ukT"][:], a["w_ukT"]).then_inc(s["f_kept"], 16)
            sp.dma_start(kept["table"][:], a["page_table"].rearrange("b p -> (b p)").unsqueeze(0)
                         ).then_inc(s["f_kept"], 16)
            sp.dma_start(kept["g_k"][:], a["g_k_col"]).then_inc(s["f_kept"], 16)
            sp.dma_start(kept["newmask"][:], a["newmask"]).then_inc(s["f_kept"], 16)

            def store(t):
                sp.wait_ge(s["f_pin"], t + 1)
                sp.dma_start(a["pin_d"][bass.ds(t * P, P), :], pin[:]).then_inc(s["f_out"], 16)
                sp.wait_ge(s["f_c"], t + 1)
                sp.dma_start(a["kv_all"][bass.ds(t * P, P), :], c_t[:]).then_inc(s["f_out"], 16)
                sp.wait_ge(s["f_kr"], t + 1)
                sp.dma_start(a["kr_all"][bass.ds(t * P, P), :], kr[:]).then_inc(s["f_out"], 16)
            with sp.Fori(0, TILES - 1) as t:
                load(t + 1)
                store(t)
            store(TILES - 1)
            sp.wait_ge(s["f_out"], 48 * TILES)
            sp.wait_ge(s["f_kept"], 64)

        @block.tensor
        def _(pe):
            pe.wait_ge(s["f_w_scaled"], CHUNKS)

            def project(t):
                pe.wait_ge(s["f_x_in"], 32 * t + 32)
                after(pe, s["f_zq"], t)
                after(pe, s["f_zck"], t)
                after(pe, s["f_pin"], t)
                for b, lo, hi in ((0, 0, QL), (1, QL, QL + KVL + ROPE), (2, QL + KVL + ROPE, IN_W)):
                    for k in range(KD):
                        mm = pe.matmul(banks[b][:, 0:hi - lo], xT[:, k, :], w_in[:, k, lo:hi],
                                       start=k == 0, stop=k == KD - 1)
                mm.then_inc(s["f_z"], 1)
                if isinstance(t, int) and t == 0:
                    pe.wait_ge(s["f_wts"], 16 * 14)
                    pe.wait_ge(s["f_w_scaled"], CHUNKS + 1)

            def rest(t, ahead):
                pe.wait_ge(s["f_zq"], t + 1)
                after(pe, s["f_ev1"], t)
                for k in range(QT):
                    mm = pe.transpose(banks[3][:, k * P:(k + 1) * P], zq[:, k * P:(k + 1) * P], ident[:])
                mm.then_inc(s["f_qlt"], 1)
                pe.wait_ge(s["f_c"], t + 1)
                after(pe, s["f_vev"], t)
                for k in range(CT):
                    mm = pe.transpose(banks[4][:, k * P:(k + 1) * P], c_t[:, k * P:(k + 1) * P], ident[:])
                mm.then_inc(s["f_ct"], 1)
                pe.wait_ge(s["f_qlT"], t + 1)
                for b in range(2):
                    for k in range(QT):
                        mm = pe.matmul(banks[5 + b][:, 0:QL], qlT[:, k, :], w_q[:, k, b * QL:(b + 1) * QL],
                                       start=k == 0, stop=k == QT - 1)
                mm.then_inc(s["f_q"], 1)
                pe.wait_ge(s["f_cT"], t + 1)
                for b, w in ((3, w_uk), (4, w_uv)):
                    for k in range(CT):
                        mm = pe.matmul(banks[b][:, :], cT[:, k, :], w[:, k, :], start=k == 0, stop=k == CT - 1)
                mm.then_inc(s["f_kv"], 1)
                ahead()
                pe.wait_ge(s["f_rot"], t + 1)
                for half, n in ((0, "f_tr0"), (1, "f_tr1")):
                    for i in range(H):
                        b = (5, 6, 7, 3)[2 * half + i // 4]
                        mm = pe.transpose(banks[b][0:HD, (i % 4) * P:(i % 4 + 1) * P], qk[:, half * H + i, :],
                                          ident[:])
                    mm.then_inc(s[n], 1)
            tiles(pe, project, rest)

        @block.scalar
        def _(act):
            act.wait_ge(s["f_consts"], 1)

            def project(t):
                act.wait_ge(s["f_x_in"], 32 * t + 32)
                after(act, s["f_ssh"], t)
                after(act, s["f_rstd"], t)
                act.activation(junk[:, 0:D], x_t[:], ACT.Square, scale=D ** -0.5,
                               accum_out=ss[:]).then_inc(s["f_sqx"], 1)
                act.wait_ge(s["f_sqx"], t + 1)
                act.activation(ss[:], ss[:], ACT.Sqrt, bias=eps[:]).then_inc(s["f_std"], 1)
                act.wait_ge(s["f_rstd"], t + 1)
                act.wait_ge(s["f_z"], t + 1)
                act.activation(zq[:], banks[0][:, 0:QL], ACT.Copy, scale=rstd[:]).then_inc(s["f_zq"], 1)
                after(act, s["f_kr"], t)
                after(act, s["f_c"], t)
                act.activation(zck[:], banks[1][:, 0:KVL + ROPE], ACT.Copy, scale=rstd[:]).then_inc(s["f_zck"], 1)

            def rest(t, ahead):
                act.wait_ge(s["f_zck"], t + 1)
                act.wait_ge(s["f_zq"], t + 1)
                after(act, s["f_rstd2"], t)
                act.activation(junk[:, 0:QL], zq[:], ACT.Square, scale=QL ** -0.5,
                               accum_out=ss2[:, 0:1]).then_inc(s["f_ms"], 1)
                act.activation(junk[:, QL:QL + KVL], zck[:, 0:KVL], ACT.Square, scale=KVL ** -0.5,
                               accum_out=ss2[:, 1:2]).then_inc(s["f_ms"], 1)
                act.wait_ge(s["f_ms"], 2 * t + 2)
                act.activation(ss2[:], ss2[:], ACT.Sqrt, bias=eps[:]).then_inc(s["f_std2"], 1)
                act.wait_ge(s["f_qlt"], t + 1)
                act.activation(qlT[:], banks[3][:, 0:QL].rearrange("p (k t) -> p k t", k=QT),
                               ACT.Copy).then_inc(s["f_qlT"], 1)
                act.wait_ge(s["f_q"], t + 1)
                act.wait_ge(s["f_rstd2"], t + 1)
                after(act, s["f_tr0"], t)
                for b in range(2):
                    act.activation(qk[:, 4 * b:4 * b + 4, :],
                                   banks[5 + b][:, 0:QL].rearrange("p (h d) -> p h d", d=HD), ACT.Copy,
                                   scale=rstd2[:, 0:1]).then_inc(s["f_qev"], 1)
                act.wait_ge(s["f_kv"], t + 1)
                after(act, s["f_tr1"], t)
                act.activation(qk[:, H:2 * H, 0:NOPE], banks[3][:, :].rearrange("p (h d) -> p h d", d=NOPE),
                               ACT.Copy).then_inc(s["f_kev"], 1)
                act.wait_ge(s["f_kev"], t + 1)
                act.wait_ge(s["f_qev"], 2 * t + 2)
                act.wait_ge(s["f_kpe"], t + 1)
                act.activation(junk[:].rearrange("p (h d) -> p h d", d=HD), qk[:], ACT.Square,
                               scale=HD ** -0.5).then_inc(s["f_sqh"], 1)
                act.wait_ge(s["f_ssh"], t + 1)
                act.activation(ssh[:], ssh[:], ACT.Sqrt, bias=eps[:]).then_inc(s["f_stdh"], 1)
                ahead()
                act.wait_ge(s["f_tr0"], t + 1)
                for b in range(2):
                    mv = act.activation(qkT[0:HD, 4 * b:4 * b + 4, bass.ds(t * P, P)],
                                        banks[5 + b][0:HD, :].rearrange("p (h t) -> p h t", t=P), ACT.Copy)
                mv.then_inc(s["f_ev0"], 1)
                act.wait_ge(s["f_tr1"], t + 1)
                for b in range(2):
                    mv = act.activation(qkT[0:HD, H + 4 * b:H + 4 * b + 4, bass.ds(t * P, P)],
                                        banks[(7, 3)[b]][0:HD, :].rearrange("p (h t) -> p h t", t=P), ACT.Copy)
                mv.then_inc(s["f_ev1"], 1)
            tiles(act, project, rest)

        @block.vector
        def _(dve):
            dve.memset(eps[:], EPS).then_inc(s["f_consts"], 1)
            dve.wait_ge(s["f_gain"], 16)
            for c in range(CHUNKS):
                dve.wait_ge(chunk_in[c], 16)
                dve.tensor_tensor(w_in[:, chunk(c), :], w_in[:, chunk(c), :],
                                  g_attn[:, chunk(c)].unsqueeze(2).to_broadcast((P, KD // CHUNKS, IN_W)),
                                  ALU.mult).then_inc(s["f_w_scaled"], 1)
            dve.wait_ge(s["f_wts"], 16 * 14)
            dve.tensor_tensor(w_q[:], w_q[:], g_ql[:].unsqueeze(2).to_broadcast((P, QT, H * HD)),
                              ALU.mult).then_inc(s["f_w_scaled"], 1)

            def project(t):
                dve.wait_ge(s["f_std"], t + 1)
                after(dve, s["f_zck"], t)
                dve.reciprocal(rstd[:], ss[:]).then_inc(s["f_rstd"], 1)
                dve.wait_ge(s["f_rstd"], t + 1)
                dve.wait_ge(s["f_z"], t + 1)
                after(dve, s["f_out"], 48 * t)
                dve.tensor_scalar(pin[:], banks[2][:, :], rstd[:], None, ALU.mult).then_inc(s["f_pin"], 1)

            def rest(t, ahead):
                rc = rope_c[:, bass.ds(t, 1), :]
                rs = rope_s[:, bass.ds(t, 1), :]
                dve.wait_ge(s["f_std2"], t + 1)
                dve.reciprocal(rstd2[:], ss2[:]).then_inc(s["f_rstd2"], 1)
                dve.wait_ge(s["f_rstd2"], t + 1)
                dve.scalar_tensor_tensor(out=c_t[:], in0=zck[:, 0:KVL], scalar=rstd2[:, 1:2], in1=g_kv[:],
                                         op0=ALU.mult, op1=ALU.mult).then_inc(s["f_c"], 1)
                dve.wait_ge(s["f_zck"], t + 1)
                dve.tensor_tensor(r_a[:, 0:1, :], zck[:, KVL:].unsqueeze(1), rc, ALU.mult).then_inc(s["f_ra"], 1)
                for i in range(2):
                    dve.tensor_tensor(r_b[:, 0:1, i * HALF:(i + 1) * HALF],
                                      zck[:, KVL + (1 - i) * HALF:KVL + (2 - i) * HALF].unsqueeze(1),
                                      rs[:, :, i * HALF:(i + 1) * HALF], ALU.mult).then_inc(s["f_rb"], 1)
                dve.wait_ge(s["f_ra"], t + 1)
                dve.wait_ge(s["f_rb"], 2 * t + 2)
                dve.tensor_tensor(kr[:], r_a[:, 0, :], r_b[:, 0, :], ALU.add).then_inc(s["f_kr"], 1)
                dve.wait_ge(s["f_ct"], t + 1)
                dve.tensor_copy(cT[:], banks[4][:, 0:KVL].rearrange("p (k t) -> p k t", k=CT)).then_inc(s["f_cT"], 1)
                dve.wait_ge(s["f_kr"], t + 1)
                after(dve, s["f_tr1"], t)
                dve.tensor_copy(qk[:, H:2 * H, NOPE:HD],
                                kr[:].unsqueeze(1).to_broadcast((P, H, ROPE))).then_inc(s["f_kpe"], 1)
                dve.wait_ge(s["f_kv"], t + 1)
                dve.tensor_copy(vall[:, bass.ds(t, 1), :], banks[4][:, :].unsqueeze(1)).then_inc(s["f_vev"], 1)
                dve.wait_ge(s["f_sqh"], t + 1)
                dve.tensor_reduce(ssh[:], junk[:].rearrange("p (h d) -> p h d", d=HD), AX,
                                  ALU.add).then_inc(s["f_ssh"], 1)
                dve.wait_ge(s["f_stdh"], t + 1)
                dve.reciprocal(rstdh[:], ssh[:]).then_inc(s["f_rstdh"], 1)
                dve.wait_ge(s["f_rstdh"], t + 1)
                dve.tensor_tensor(qk[:], qk[:], rstdh[:].unsqueeze(2).to_broadcast((P, 2 * H, HD)),
                                  ALU.mult).then_inc(s["f_n1"], 1)
                dve.wait_ge(s["f_n1"], t + 1)
                for i in range(2):
                    dve.tensor_tensor(qk[:, i * H:(i + 1) * H, :], qk[:, i * H:(i + 1) * H, :],
                                      g_qk[:, i:i + 1, :].to_broadcast((P, H, HD)), ALU.mult).then_inc(s["f_n2"], 1)
                dve.wait_ge(s["f_n2"], 2 * t + 2)
                dve.tensor_tensor(r_a[:], qk[:, 0:H, NOPE:HD], rc.to_broadcast((P, H, ROPE)),
                                  ALU.mult).then_inc(s["f_qra"], 1)
                for i in range(2):
                    dve.tensor_tensor(r_b[:, :, i * HALF:(i + 1) * HALF],
                                      qk[:, 0:H, NOPE + (1 - i) * HALF:NOPE + (2 - i) * HALF],
                                      rs[:, :, i * HALF:(i + 1) * HALF].to_broadcast((P, H, HALF)),
                                      ALU.mult).then_inc(s["f_qrb"], 1)
                dve.wait_ge(s["f_qra"], t + 1)
                dve.wait_ge(s["f_qrb"], 2 * t + 2)
                dve.tensor_tensor(qk[:, 0:H, NOPE:HD], r_a[:], r_b[:], ALU.add).then_inc(s["f_rot"], 1)
                ahead()
            tiles(dve, project, rest)


def prompt_attention(nc, a, qkT, vall):
    with ExitStack() as ctx:
        def sb(name, shape, dt=F32):
            return ctx.enter_context(nc.sbuf_tensor(name, shape, dt))

        ident = sb("a_ident", [P, P])
        causal = sb("a_causal", [P, P])
        q_now = [sb(f"a_q{e}", [HD, P]) for e in range(2)]
        prob = [sb(f"a_p{e}", [P, SEQ]) for e in range(2)]
        probT = [sb(f"a_pT{e}", [P, PT_TILES, P]) for e in range(2)]
        mx = [sb(f"a_mx{e}", [P, 1]) for e in range(2)]
        nmx = [sb(f"a_nmx{e}", [P, 1]) for e in range(2)]
        tot = [sb(f"a_tot{e}", [P, 1]) for e in range(2)]
        inv = [sb(f"a_inv{e}", [P, 1]) for e in range(2)]
        o_all = sb("a_o", [P, H * VD])
        oT = sb("a_oT", [P, G4, P])
        score = [ctx.enter_context(nc.psum_tensor(f"a_s{e}", [P, SEQ], F32)) for e in range(2)]
        turn = [ctx.enter_context(nc.psum_tensor(f"a_t{e}", [P, 512], F32)) for e in range(2)]
        out_b = [ctx.enter_context(nc.psum_tensor(f"a_op{e}", [P, 512], F32)) for e in range(2)]
        out = [b[:, 0:VD] for b in out_b]
        out_turn = out_b[1]
        s = with_sems(nc, ctx, """a_in a_qc a_s a_mask a_mx a_nmx a_exp a_tr a_pt a_pv a_inv a_o a_ot a_otev
            a_st""")
        block = ctx.enter_context(nc.Block())
        PAIRS = H // 2
        LAST = PT_TILES - 1

        def batches(i):
            return [range(b, min(b + 4, i + 1)) for b in range(0, i + 1, 4)]

        def batch_number(i, h, b):
            before = sum(H * len(batches(j)) for j in range(i))
            return before + h * len(batches(i)) + b

        def less_one(count, i, later):
            return count - 1 if i or later else count

        def heads(eng, start, finish, row_end, finish_first=False):
            def step(head, following):
                parts = [lambda: start(*following) if following else None, lambda: finish(*head)]
                for part in reversed(parts) if finish_first else parts:
                    part()
            start(0, 0, 0)
            for i in range(PT_TILES):
                with eng.Fori(0, PAIRS - 1) as m:
                    step((i, 2 * m, 0), (i, 2 * m + 1, 1))
                    step((i, 2 * m + 1, 1), (i, 2 * m + 2, 0))
                step((i, H - 2, 0), (i, H - 1, 1))
                step((i, H - 1, 1), (i + 1, 0, 0) if i < LAST else None)
                row_end(i)

        @block.sync
        def _(sp):
            sp.dma_start(ident[:], a["ident"]).then_inc(s["a_in"], 16)
            sp.dma_start(causal[:], a["causal"]).then_inc(s["a_in"], 16)
            for i in range(PT_TILES):
                sp.wait_ge(s["a_otev"], i + 1)
                sp.dma_start(a["mixT_d"][:, :, i * P:(i + 1) * P], oT[:]).then_inc(s["a_st"], 16)
            sp.wait_ge(s["a_st"], 16 * PT_TILES)

        @block.gpsimd
        def _(pool):
            for i in range(PT_TILES):
                with pool.Fori(0, PAIRS) as m:
                    for e in range(2):
                        n = i * H + 2 * m + e
                        pool.wait_ge(s["a_s"], less_one(n, i, e))
                        pool.tensor_copy(q_now[e][:].unsqueeze(1),
                                         qkT[0:HD, bass.ds(2 * m + e, 1), i * P:(i + 1) * P]).then_inc(s["a_qc"], 1)

        @block.tensor
        def _(pe):
            pe.wait_ge(s["a_in"], 32)

            def start(i, h, e):
                n, L = i * H + h, (i + 1) * P
                pe.wait_ge(s["a_qc"], n + 1)
                if i or not isinstance(h, int) or h:
                    pe.wait_ge(s["a_exp"], n - 1)
                for c in range(0, L, 512):
                    w = min(512, L - c)
                    mm = pe.matmul(score[e][:, c:c + w], q_now[e][:], qkT[0:HD, bass.ds(H + h, 1), c:c + w],
                                   start=True, stop=True)
                mm.then_inc(s["a_s"], 1)

            def finish(i, h, e):
                n = i * H + h
                pe.wait_ge(s["a_exp"], n + 1)
                for b, blocks in enumerate(batches(i)):
                    g = batch_number(i, h, b)
                    bank = (e * len(batches(i)) + b) % 2
                    pe.wait_ge(s["a_pt"], less_one(g, i, e or b))
                    for k in blocks:
                        mm = pe.transpose(turn[bank][:, (k % 4) * P:(k % 4 + 1) * P], prob[e][:, k * P:(k + 1) * P],
                                          ident[:])
                    mm.then_inc(s["a_tr"], 1)
                pe.wait_ge(s["a_o"], less_one(n, i, e))
                if e == 1:
                    after(pe, s["a_otev"], i)
                for k in range(i + 1):
                    if k % 4 == 0:
                        pe.wait_ge(s["a_pt"], batch_number(i, h, k // 4) + 1)
                    mm = pe.matmul(out[e], probT[e][:, k, :], vall[:, k, bass.ds(h * VD, VD)], start=k == 0,
                                   stop=k == i)
                mm.then_inc(s["a_pv"], 1)

            def row_end(i):
                pe.wait_ge(s["a_o"], H * (i + 1))
                for k in range(G4):
                    mm = pe.transpose(out_turn[:, k * P:(k + 1) * P], o_all[:, k * P:(k + 1) * P], ident[:])
                mm.then_inc(s["a_ot"], 1)
            heads(pe, start, finish, row_end)

        @block.scalar
        def _(act):
            def start(i, h, e):
                n, L = i * H + h, (i + 1) * P
                act.wait_ge(s["a_nmx"], n + 1)
                if i or not isinstance(h, int) or h:
                    act.wait_ge(s["a_inv"], n - 1)
                act.activation(prob[e][:, 0:L], score[e][:, 0:L], ACT.Exp, bias=nmx[e][:], scale=SM,
                               accum_out=tot[e][:]).then_inc(s["a_exp"], 1)

            def finish(i, h, e):
                n = i * H + h
                act.wait_ge(s["a_pv"], less_one(n, i, e))
                for b, blocks in enumerate(batches(i)):
                    bank = (e * len(batches(i)) + b) % 2
                    act.wait_ge(s["a_tr"], batch_number(i, h, b) + 1)
                    act.activation(probT[e][:, 4 * b:4 * b + len(blocks), :],
                                   turn[bank][:, 0:len(blocks) * P].rearrange("p (k t) -> p k t", t=P),
                                   ACT.Copy).then_inc(s["a_pt"], 1)

            def row_end(i):
                act.wait_ge(s["a_ot"], i + 1)
                after(act, s["a_st"], 16 * i)
                act.activation(oT[:], out_turn[:, :].rearrange("p (k t) -> p k t", t=P),
                               ACT.Copy).then_inc(s["a_otev"], 1)
            heads(act, start, finish, row_end, finish_first=True)

        @block.vector
        def _(dve):
            dve.wait_ge(s["a_in"], 32)

            def start(i, h, e):
                n, L = i * H + h, (i + 1) * P
                dve.wait_ge(s["a_s"], n + 1)
                dve.tensor_tensor(score[e][:, L - P:L], score[e][:, L - P:L], causal[:],
                                  ALU.add).then_inc(s["a_mask"], 1)
                dve.wait_ge(s["a_mask"], n + 1)
                dve.tensor_reduce(mx[e][:], score[e][:, 0:L], AX, ALU.max).then_inc(s["a_mx"], 1)
                dve.wait_ge(s["a_mx"], n + 1)
                if i or not isinstance(h, int) or h:
                    dve.wait_ge(s["a_exp"], n - 1)
                dve.tensor_scalar(nmx[e][:], mx[e][:], -SM, None, ALU.mult).then_inc(s["a_nmx"], 1)

            def finish(i, h, e):
                n = i * H + h
                dve.wait_ge(s["a_exp"], n + 1)
                dve.reciprocal(inv[e][:], tot[e][:]).then_inc(s["a_inv"], 1)
                after(dve, s["a_ot"], i)
                dve.wait_ge(s["a_inv"], n + 1)
                dve.wait_ge(s["a_pv"], n + 1)
                dve.tensor_scalar(o_all[:, bass.ds(h * VD, VD)], out[e], inv[e][:], None,
                                  ALU.mult).then_inc(s["a_o"], 1)
            heads(dve, start, finish, lambda i: None)


def sample_attention(nc, a, qkT, kept):
    SQ = DEC_S * H
    with ExitStack() as ctx:
        def sb(name, shape, dt=F32):
            return ctx.enter_context(nc.sbuf_tensor(name, shape, dt))

        ident, w_uk, w_uv, w_ukT, g_k, newmask, table = (
            kept[n] for n in ("ident", "w_uk", "w_uv", "w_ukT", "g_k", "newmask", "table"))
        eps = sb("d_eps", [P, 1])
        qg = sb("d_qg", [NOPE, H, NS])
        qr = sb("d_qr", [ROPE, H, NS])
        qa = sb("d_qa", [P, CT, H, NS])
        page = [sb(f"d_page{e}", [P, PAGES, KVL + ROPE]) for e in range(2)]
        latent_rows = [sb(f"d_latent{e}", [P, PAGES, KVL]) for e in range(2)]
        krT = [sb(f"d_krT{e}", [ROPE, PAGES, P]) for e in range(2)]
        k_new = sb("d_k_new", [HD, H, DEC_S])
        c_now = [sb(f"d_c_now{e}", [DEC_S, KVL]) for e in range(2)]
        sq = [sb(f"d_sq{e}", [P, H * NOPE]) for e in range(2)]
        krsq = sb("d_krsq", [P, PAGES, ROPE])
        krss = sb("d_krss", [P, PAGES])
        kss2 = [sb(f"d_kss{e}", [P, PAGES, H]) for e in range(2)]
        s_all2 = [sb(f"d_s{e}", [P, PAGES + 1, SQ]) for e in range(2)]
        rows = sb("d_rows", [P, PAST + DEC_S])
        s_row = rows[0:SQ, :]
        mx = sb("d_mx", [SQ, 1])
        nmx = sb("d_nmx", [SQ, 1])
        tot = sb("d_tot", [SQ, 1])
        inv = sb("d_inv", [SQ, 1])
        pT = sb("d_pT", [P, PAGES + 1, SQ])
        ol = sb("d_ol", [SQ, KVL])
        olT = sb("d_olT", [P, CT, H, NS])
        o = rows[0:NS, 0:H * VD]
        oT = rows[:, 512:512 + G4 * P].rearrange("p (k t) -> p k t", k=G4)
        bank = lambda n: ctx.enter_context(nc.psum_tensor(n, [P, 512], F32))
        kn = [bank("d_kn0"), bank("d_kn1")]
        st = [bank("d_st0"), bank("d_st1")]
        misc = [bank("d_m0"), bank("d_m1")]
        new = bank("d_new")
        lat = bank("d_lat")
        s = with_sems(nc, ctx, """d_first0 d_first1 d_rest0 d_rest1 d_lt0 d_lt1 d_eps d_qg d_qap d_qa d_mm d_sq d_red d_sev d_krsq d_krss
            d_ks1 d_ks2 d_ks3 d_s1 d_knew d_new d_smask d_tr d_row d_mx d_nmx d_exp d_inv d_ptr d_pt d_lat d_ol
            d_olt d_olT d_op d_o d_ot d_zero d_oT d_st""")
        first_in = [s["d_first0"], s["d_first1"]]
        rest_in = [s["d_rest0"], s["d_rest1"]]
        FIRST = 4
        ROTARY = 12
        latent_in = [s["d_lt0"], s["d_lt1"]]
        n_phys = a["page"].shape[0]
        block = ctx.enter_context(nc.Block())

        def sequences(eng, begin, pages, tail):
            def one(b, e, n, before):
                begin(b)
                pages(b, e, n, before)
            one(0, 0, 1, {})
            with eng.Fori(0, DEC_B // 2 - 1) as m:
                one(2 * m + 1, 1, m + 1, tail(2 * m, 0, m + 1))
                one(2 * m + 2, 0, m + 2, tail(2 * m + 1, 1, m + 1))
            one(DEC_B - 1, 1, DEC_B // 2, tail(DEC_B - 2, 0, DEC_B // 2))
            for step in tail(DEC_B - 1, 1, DEC_B // 2).values():
                step()

        @block.sync
        def _(sp):
            def each_page(b):
                for p in range(PAGES):
                    yield p, sp.value_load(table[0:1, bass.ds(b * PAGES + p, 1)], min_val=0, max_val=n_phys - 1)

            def load_keys(b, e):
                for p, phys in each_page(b):
                    done = first_in[e] if p < FIRST else rest_in[e]
                    for dst, src in ((page[e], a["page"]), (krT[e], a["page_krT"])):
                        sp.dma_start(dst[:, p, :], src[bass.ds(phys, 1)].rearrange("o p c -> (o p) c")
                                     ).then_inc(done, 16)

            def load_latents(b, e):
                sp.dma_start(c_now[e][:], a["kv_all"][bass.ds(SEQ + b * DEC_S, DEC_S), :]).then_inc(latent_in[e], 16)
                for p, phys in each_page(b):
                    sp.dma_start(latent_rows[e][:, p, :], a["page_rows"][bass.ds(phys, 1)]
                                 .rearrange("o p c -> (o p) c")).then_inc(latent_in[e], 16)
            load_keys(0, 0)
            load_keys(1, 1)
            load_latents(0, 0)
            load_latents(1, 1)
            with sp.Fori(0, DEC_B // 2 - 1) as m:
                for e in range(2):
                    n = 2 * m + e + 1
                    sp.wait_ge(s["d_s1"], n)
                    load_keys(n + 1, e)
                    sp.wait_ge(s["d_lat"], n)
                    load_latents(n + 1, e)
            sp.wait_ge(s["d_oT"], 1)
            sp.dma_start(a["mixT_d"][:, :, SEQ:NPAD], oT).then_inc(s["d_st"], 16)
            sp.wait_ge(s["d_st"], 16)

        @block.tensor
        def _(pe):
            pe.wait_ge(s["d_qg"], 2)
            for k in range(CT):
                for h in range(H):
                    mm = pe.matmul(kn[k][:, h * NS:(h + 1) * NS], w_ukT[:, h, k * P:(k + 1) * P], qg[:, h, :],
                                   start=True, stop=True)
            mm.then_inc(s["d_qap"], 1)
            pe.wait_ge(s["d_qa"], 2)

            def pages(b, e, n, tail):
                cols = bass.ds(b * DEC_S, DEC_S)
                for p in range(PAGES):
                    if p == 0:
                        pe.wait_ge(first_in[e], 32 * FIRST * n)
                    elif p == FIRST:
                        pe.wait_ge(rest_in[e], 32 * (PAGES - FIRST) * n)
                    after(pe, s["d_sq"], b * PAGES + p - 1)
                    after(pe, s["d_sev"], b * PAGES + p - 1)
                    for k in range(CT):
                        pe.matmul(kn[p % 2][:, :], page[e][:, p, k * P:(k + 1) * P], w_uk[:, k, :],
                                  start=k == 0, stop=k == CT - 1)
                    for k in range(CT):
                        pe.matmul(st[p % 2][:, 0:SQ].rearrange("p (h t) -> p h t", t=DEC_S),
                                  page[e][:, p, k * P:(k + 1) * P], qa[:, k, :, cols], start=k == 0, stop=False)
                    mm = pe.matmul(st[p % 2][:, 0:SQ].rearrange("p (h t) -> p h t", t=DEC_S),
                                   krT[e][:, p, :], qr[:, :, cols], start=False, stop=True)
                    mm.then_inc(s["d_mm"], 1)
                    if p == 0:
                        pe.wait_ge(s["d_knew"], b + 1)
                        after(pe, s["d_smask"], b)
                        for h in range(H):
                            mm = pe.matmul(new[0:DEC_S, h * DEC_S:(h + 1) * DEC_S], k_new[:, h, :],
                                           qkT[0:HD, h, bass.ds(SEQ + b * DEC_S, DEC_S)], start=True, stop=True)
                        mm.then_inc(s["d_new"], 1)
                    if p in tail:
                        tail[p]()

            def tail(t, e, n):
                s_all = s_all2[e]

                def turn_first():
                    pe.wait_ge(s["d_s1"], t + 1)
                    pe.wait_ge(s["d_smask"], t + 1)
                    pe.wait_ge(s["d_olT"], t)
                    pe.wait_ge(s["d_pt"], 2 * t)
                    turn(0)
                    turn(1)

                def turn(c):
                    for p in range(4 * c, 4 * c + 4):
                        mm = pe.transpose(misc[c % 2][0:SQ, (p % 4) * P:(p % 4 + 1) * P], s_all[:, p, :], ident[:])
                    mm.then_inc(s["d_tr"], 1)

                def turn_rest():
                    for c in (2, 3):
                        pe.wait_ge(s["d_row"], 5 * t + c - 1)
                        turn(c)
                    pe.transpose(new[0:SQ, 2 * SQ:2 * SQ + DEC_S], s_all[0:DEC_S, PAGES, :],
                                 ident[0:DEC_S, 0:DEC_S]).then_inc(s["d_tr"], 1)

                def probs():
                    pe.wait_ge(s["d_exp"], t + 1)
                    for p in range(PAGES):
                        mm = pe.matmul(misc[0][:, p * SQ:(p + 1) * SQ], s_row[:, p * P:(p + 1) * P],
                                       ident[0:SQ, 0:SQ], start=True, stop=True)
                    mm.then_inc(s["d_ptr"], 1)
                    pe.transpose(misc[1][0:DEC_S, 0:SQ], s_row[:, PAST:PAST + DEC_S],
                                 ident[0:SQ, 0:SQ]).then_inc(s["d_ptr"], 1)

                def latent():
                    pe.wait_ge(latent_in[e], 16 * (PAGES + 1) * n)
                    pe.wait_ge(s["d_pt"], 2 * t + 2)
                    for p in range(PAGES):
                        pe.matmul(lat[0:SQ, 0:KVL], pT[:, p, :], latent_rows[e][:, p, :], start=p == 0, stop=False)
                    pe.matmul(lat[0:SQ, 0:KVL], pT[0:DEC_S, PAGES, :], c_now[e][:], start=False,
                              stop=True).then_inc(s["d_lat"], 1)

                def latent_turn():
                    pe.wait_ge(s["d_ol"], t + 1)
                    for k in range(CT):
                        mm = pe.matmul(misc[0][:, k * SQ:(k + 1) * SQ], ol[:, k * P:(k + 1) * P],
                                       ident[0:SQ, 0:SQ], start=True, stop=True)
                    mm.then_inc(s["d_olt"], 1)
                return {1: turn_first, 2: turn_rest, 6: probs, 7: latent, 9: latent_turn}
            sequences(pe, lambda b: None, pages, tail)
            pe.wait_ge(s["d_olT"], DEC_B)
            for h in range(H):
                for k in range(CT):
                    mm = pe.matmul(lat[0:NS, h * VD:(h + 1) * VD], olT[:, k, h, :], w_uv[:, k, h * VD:(h + 1) * VD],
                                   start=k == 0, stop=k == CT - 1)
            mm.then_inc(s["d_op"], 1)
            pe.wait_ge(s["d_o"], 1)
            for k in range(G4):
                mm = pe.transpose(new[:, k * NS:(k + 1) * NS], o[:, k * P:(k + 1) * P], ident[0:NS, 0:NS])
            mm.then_inc(s["d_ot"], 1)

        @block.scalar
        def _(act):
            act.wait_ge(s["d_eps"], 1)
            act.wait_ge(s["d_qap"], 1)
            for k in range(CT):
                act.activation(qa[:, k, :, :], kn[k][:, 0:H * NS].rearrange("p (h t) -> p h t", t=NS),
                               ACT.Copy).then_inc(s["d_qa"], 1)

            def pages(b, e, n, tail):
                for p in range(PAGES):
                    if p == ROTARY:
                        act.wait_ge(first_in[e], 32 * FIRST * n)
                        act.wait_ge(rest_in[e], 32 * (PAGES - FIRST) * n)
                        after(act, s["d_krss"], b)
                        act.activation(krsq[:], page[e][:, :, KVL:], ACT.Square,
                                       scale=HD ** -0.5).then_inc(s["d_krsq"], 1)
                    if p in tail:
                        tail[p]()
                    act.wait_ge(s["d_mm"], b * PAGES + p + 1)
                    after(act, s["d_red"], b * PAGES + p - 1)
                    act.activation(sq[p % 2][:], kn[p % 2][:, :], ACT.Square,
                                   scale=HD ** -0.5).then_inc(s["d_sq"], 1)
                act.wait_ge(s["d_ks1"], b + 1)
                act.activation(kss2[e][:], kss2[e][:], ACT.Sqrt, bias=eps[:]).then_inc(s["d_ks2"], 1)

            def tail(t, e, n):
                def row(c):
                    act.wait_ge(s["d_tr"], 5 * t + c + 1)
                    if c == 0:
                        act.wait_ge(s["d_ptr"], 2 * t)
                    w = 512 if c < 4 else DEC_S
                    act.activation(s_row[:, 512 * c:512 * c + w],
                                   misc[c % 2][0:SQ, 0:w] if c < 4 else new[0:SQ, 2 * SQ:2 * SQ + w],
                                   ACT.Copy).then_inc(s["d_row"], 1)

                def rows_first():
                    row(0)
                    row(1)

                def rows_rest():
                    for c in (2, 3, 4):
                        row(c)

                def exp():
                    act.wait_ge(s["d_row"], 5 * t + 5)
                    act.wait_ge(s["d_nmx"], t + 1)
                    act.wait_ge(s["d_inv"], t)
                    act.activation(s_row, s_row, ACT.Exp, bias=nmx[:], scale=SM,
                                   accum_out=tot[:]).then_inc(s["d_exp"], 1)

                def probs():
                    act.wait_ge(s["d_lat"], t)
                    act.wait_ge(s["d_ptr"], 2 * t + 1)
                    act.activation(pT[:, 0:PAGES, :], misc[0][:, :].rearrange("p (k t) -> p k t", t=SQ),
                                   ACT.Copy).then_inc(s["d_pt"], 1)
                    act.wait_ge(s["d_ptr"], 2 * t + 2)
                    act.activation(pT[0:DEC_S, PAGES, :], misc[1][0:DEC_S, 0:SQ], ACT.Copy).then_inc(s["d_pt"], 1)

                def latent_turn():
                    act.wait_ge(s["d_olt"], t + 1)
                    act.activation(olT[:, :, :, bass.ds(t * DEC_S, DEC_S)],
                                   misc[0][:, 0:CT * SQ].rearrange("p (k h t) -> p k h t", k=CT, h=H),
                                   ACT.Copy).then_inc(s["d_olT"], 1)
                return {2: rows_first, 3: rows_rest, 5: exp, 7: probs, 10: latent_turn}
            sequences(act, lambda b: None, pages, tail)
            act.wait_ge(s["d_op"], 1)
            act.activation(o, lat[0:NS, :], ACT.Copy).then_inc(s["d_o"], 1)
            act.wait_ge(s["d_ot"], 1)
            act.wait_ge(s["d_zero"], 1)
            act.activation(oT[:, :, 0:NS], new[:, 0:G4 * NS].rearrange("p (k t) -> p k t", t=NS),
                           ACT.Copy).then_inc(s["d_oT"], 1)

        @block.vector
        def _(dve):
            dve.memset(eps[:], EPS).then_inc(s["d_eps"], 1)
            dve.tensor_scalar(qg[:], qkT[0:NOPE, 0:H, SEQ:NT], g_k[0:NOPE, :], None, ALU.mult).then_inc(s["d_qg"], 1)
            dve.tensor_scalar(qr[:], qkT[NOPE:HD, 0:H, SEQ:NT], g_k[NOPE:HD, :], None,
                              ALU.mult).then_inc(s["d_qg"], 1)

            def begin(b):
                after(dve, s["d_new"], b)
                dve.tensor_copy(k_new[:], qkT[0:HD, H:2 * H, bass.ds(SEQ + b * DEC_S, DEC_S)]).then_inc(s["d_knew"], 1)
                after(dve, s["d_tr"], 5 * (b - 1))

            def pages(b, e, n, tail):
                kss, s_all = kss2[e], s_all2[e]
                for p in range(PAGES):
                    if p == ROTARY + 1:
                        dve.wait_ge(s["d_krsq"], b + 1)
                        after(dve, s["d_ks1"], b)
                        dve.tensor_reduce(krss[:], krsq[:], AX, ALU.add).then_inc(s["d_krss"], 1)
                    if p in tail:
                        tail[p]()
                    dve.wait_ge(s["d_mm"], b * PAGES + p + 1)
                    dve.tensor_copy(s_all[:, p, :], st[p % 2][:, 0:SQ]).then_inc(s["d_sev"], 1)
                    dve.wait_ge(s["d_sq"], b * PAGES + p + 1)
                    dve.tensor_reduce(kss[:, p, :], sq[p % 2][:].rearrange("p (h n) -> p h n", n=NOPE), AX,
                                      ALU.add).then_inc(s["d_red"], 1)
                dve.wait_ge(s["d_red"], (b + 1) * PAGES)
                dve.wait_ge(s["d_krss"], b + 1)
                dve.tensor_tensor(kss[:], kss[:], krss[:].unsqueeze(2).to_broadcast((P, PAGES, H)),
                                  ALU.add).then_inc(s["d_ks1"], 1)
                dve.wait_ge(s["d_new"], b + 1)
                dve.tensor_tensor(s_all[0:DEC_S, PAGES, :].rearrange("p (h t) -> p h t", t=DEC_S),
                                  new[0:DEC_S, 0:SQ].rearrange("p (h t) -> p h t", t=DEC_S), newmask[:],
                                  ALU.add).then_inc(s["d_smask"], 1)
                dve.wait_ge(s["d_ks2"], b + 1)
                dve.reciprocal(kss[:], kss[:]).then_inc(s["d_ks3"], 1)
                dve.wait_ge(s["d_ks3"], b + 1)
                dve.wait_ge(s["d_sev"], (b + 1) * PAGES)
                sv = s_all[:, 0:PAGES, :].rearrange("p k (h t) -> p (k h) t", t=DEC_S)
                dve.tensor_tensor(sv, sv, kss[:].rearrange("p k h -> p (k h)").unsqueeze(2)
                                  .to_broadcast((P, PAGES * H, DEC_S)), ALU.mult).then_inc(s["d_s1"], 1)

            def tail(t, e, n):
                def maximum():
                    dve.wait_ge(s["d_row"], 5 * t + 5)
                    dve.tensor_reduce(mx[:], s_row, AX, ALU.max).then_inc(s["d_mx"], 1)
                    dve.wait_ge(s["d_mx"], t + 1)
                    dve.wait_ge(s["d_exp"], t)
                    dve.tensor_scalar(nmx[:], mx[:], -SM, None, ALU.mult).then_inc(s["d_nmx"], 1)

                def latent():
                    dve.wait_ge(s["d_exp"], t + 1)
                    dve.reciprocal(inv[:], tot[:]).then_inc(s["d_inv"], 1)
                    dve.wait_ge(s["d_inv"], t + 1)
                    dve.wait_ge(s["d_lat"], t + 1)
                    dve.wait_ge(s["d_olt"], t)
                    dve.tensor_scalar(ol[:], lat[0:SQ, 0:KVL], inv[:], None, ALU.mult).then_inc(s["d_ol"], 1)
                return {4: maximum, 9: latent}
            sequences(dve, begin, pages, tail)
            dve.wait_ge(s["d_ptr"], 2 * DEC_B)
            dve.memset(oT, 0.0).then_inc(s["d_zero"], 1)


def mixer_out(nc, a, h2_parts):
    with ExitStack() as ctx:
        def sb(name, shape, dt=F32):
            return ctx.enter_context(nc.sbuf_tensor(name, shape, dt))

        ident = sb("o_ident", [P, P])
        band = sb("o_band", [P, 5, G4, P])
        w_pool = sb("o_w_pool", [P, G4, P])
        scale = sb("o_scale", [P, G4])
        w_o = sb("o_w_o", [P, KD, D])
        g_ffn = sb("o_g_ffn", [P, KD])
        eps = sb("o_eps", [P, 1])
        x_t = sb("o_x", [P, D])
        rows_now = sb("o_rows", [P, PW])
        rows_old = sb("o_rows_old", [P, PW])
        mT = sb("o_mT", [P, KD, P])
        pooled = sb("o_pooled", [P, G4, P])
        x1 = sb("o_x1", [P, D])
        h2 = sb("o_h2", [P, D])
        h2T = sb("o_h2T", [P, KD, P])
        h2h, h2l = h2_parts
        ss = sb("o_ss", [P, 1])
        rstd = sb("o_rstd", [P, 1])
        bank = lambda n: ctx.enter_context(nc.psum_tensor(n, [P, 512], F32))
        pool_b, mix_b = bank("o_pb"), bank("o_mb")
        out_b = [bank("o_o0"), bank("o_o1")]
        turn_b = [bank("o_t0"), bank("o_t1")]
        s = with_sems(nc, ctx, """o_wts o_wo0 o_wo1 o_late o_eps o_rows_in o_mix_in o_x_in o_pl o_plev o_y o_yev o_mm o_x1 o_sq o_std o_rstd o_h2 o_tr
            o_h2T o_hh o_hl o_st o_pool""")
        block = ctx.enter_context(nc.Block())

        def tiles(eng, pool, rest):
            pool(0, 0, None)
            with eng.Fori(0, PT_TILES - 2) as t:
                rest(t, lambda: pool(t + 1, 1, 2))
            rest(PT_TILES - 2, lambda: pool(PT_TILES - 1, 1, 2))
            rest(PT_TILES - 1, lambda: pool(PT_TILES, 3, 4))
            rest(PT_TILES, lambda: None)

        half_in = [s["o_wo0"], s["o_wo1"]]

        def columns(t):
            return bass.ds(t * P, NS if isinstance(t, int) and t == PT_TILES else P)

        def load_rows(eng, t):
            eng.dma_start(rows_now[:], a["pin_d"][bass.ds(t * P, P), :]).then_inc(s["o_rows_in"], 16)
            inner = not isinstance(t, int) or 0 < t < PT_TILES
            older = a["pin_d"][bass.ds((t - 1) * P, P), :] if inner else a["state"]
            eng.dma_start(rows_old[:], older).then_inc(s["o_rows_in"], 16)

        @block.sync
        def _(sp):
            load_rows(sp, 0)
            for dst, src in ((band, "band"), (w_pool, "w_pool"), (scale, "pool_scale")):
                sp.dma_start(dst[:], a[src]).then_inc(s["o_wts"], 16)

            def pool(t, now, old):
                after(sp, s["o_x1"], 2 * t)
                sp.dma_start(mT[:, 0:G4, :], a["mixT_d"][:, :, bass.ds(t * P, P)]).then_inc(s["o_mix_in"], 16)
                sp.dma_start(x_t[:], a["x"][bass.ds(t * P, P), :]).then_inc(s["o_x_in"], 16)
                if isinstance(t, int) and t == 0:
                    for n in range(2):
                        sp.dma_start(w_o[:, :, n * 512:(n + 1) * 512],
                                     a["w_o"][:, :, n * 512:(n + 1) * 512]).then_inc(half_in[n], 16)
                        if n == 0:
                            sp.dma_start(ident[:], a["ident"]).then_inc(s["o_late"], 16)
                            sp.dma_start(g_ffn[:], a["g_ffn"]).then_inc(s["o_late"], 16)

            def rest(t, ahead):
                ahead()
                sp.wait_ge(s["o_h2"], t + 1)
                sp.dma_start(a["x1_d"][bass.ds(t * P, P), :], x1[:]).then_inc(s["o_st"], 16)
            tiles(sp, pool, rest)
            sp.dma_start(a["pool_prompt"], a["pin_d"][SEQ - PSTATE:SEQ, :]).then_inc(s["o_pool"], 16)
            sp.dma_start(a["pool_sample"][:, 0:PSTATE - DEC_S, :],
                         a["state_pool"][:, DEC_S:PSTATE, :]).then_inc(s["o_pool"], 16)
            sp.dma_start(a["pool_sample"][:, PSTATE - DEC_S:PSTATE, :],
                         a["pin_d"][SEQ:NT, :].rearrange("(b t) c -> b t c", t=DEC_S)).then_inc(s["o_pool"], 16)
            sp.wait_ge(s["o_st"], 16 * TILES)
            sp.wait_ge(s["o_pool"], 48)

        @block.tensor
        def _(pe):
            pe.wait_ge(s["o_wts"], 48)

            def pool(t, now, old):
                pe.wait_ge(s["o_rows_in"], 32 * t + 32)
                after(pe, s["o_plev"], t)
                for g in range(G4):
                    mm = pe.matmul(pool_b[:, g * P:(g + 1) * P], rows_now[:, g * P:(g + 1) * P], band[:, now, g, :],
                                   start=True, stop=old is None)
                    if old is not None:
                        mm = pe.matmul(pool_b[:, g * P:(g + 1) * P], rows_old[:, g * P:(g + 1) * P],
                                       band[:, old, g, :], start=False, stop=True)
                mm.then_inc(s["o_pl"], 1)
                pe.wait_ge(s["o_plev"], t + 1)
                after(pe, s["o_yev"], t)
                for g in range(G4):
                    mm = pe.matmul(mix_b[:, g * P:(g + 1) * P], w_pool[:, g, :], pooled[:, g, :], start=True,
                                   stop=True)
                mm.then_inc(s["o_y"], 1)

            def rest(t, ahead):
                pe.wait_ge(s["o_mix_in"], 16 * t + 16)
                after(pe, s["o_x1"], 2 * t)
                pe.wait_ge(s["o_yev"], t + 1)
                for n in range(2):
                    pe.wait_ge(half_in[n], 16)
                    for k in range(KD):
                        mm = pe.matmul(out_b[n][:, :], mT[:, k, :], w_o[:, k, n * 512:(n + 1) * 512], start=k == 0,
                                       stop=k == KD - 1)
                mm.then_inc(s["o_mm"], 1)
                ahead()
                pe.wait_ge(s["o_late"], 32)
                pe.wait_ge(s["o_h2"], t + 1)
                after(pe, s["o_h2T"], 2 * t)
                for k in range(KD):
                    mm = pe.transpose(turn_b[k // 4][:, (k % 4) * P:(k % 4 + 1) * P], h2[:, k * P:(k + 1) * P],
                                      ident[:])
                mm.then_inc(s["o_tr"], 1)
            tiles(pe, pool, rest)

        @block.scalar
        def _(act):
            act.wait_ge(s["o_eps"], 1)

            def pool(t, now, old):
                act.wait_ge(s["o_pl"], t + 1)
                after(act, s["o_y"], t)
                act.activation(pooled[:], pool_b[:, :].rearrange("p (g t) -> p g t", g=G4),
                               ACT.Copy).then_inc(s["o_plev"], 1)
                if not isinstance(t, int) or t < PT_TILES:
                    load_rows(act, t + 1)

            def rest(t, ahead):
                ahead()
                act.wait_ge(s["o_x1"], 2 * t + 2)
                after(act, s["o_rstd"], t)
                after(act, s["o_tr"], t)
                act.activation(h2[:], x1[:], ACT.Square, scale=D ** -0.5, accum_out=ss[:]).then_inc(s["o_sq"], 1)
                act.wait_ge(s["o_sq"], t + 1)
                act.activation(ss[:], ss[:], ACT.Sqrt, bias=eps[:]).then_inc(s["o_std"], 1)
                act.wait_ge(s["o_rstd"], t + 1)
                act.activation(h2[:], x1[:], ACT.Copy, scale=rstd[:]).then_inc(s["o_h2"], 1)
                act.wait_ge(s["o_h2T"], 2 * t + 2)
                n = NS if isinstance(t, int) and t == PT_TILES else P
                act.activation(h2h[:, :, columns(t)], h2T[:, :, 0:n], ACT.Copy).then_inc(s["o_hh"], 1)
            tiles(act, pool, rest)

        @block.gpsimd
        def _(gpsimd):
            def rest(t, ahead):
                n = NS if isinstance(t, int) and t == PT_TILES else P
                gpsimd.wait_ge(s["o_hh"], t + 1)
                gpsimd.tensor_tensor(h2l[:, :, columns(t)], h2T[:, :, 0:n], h2h[:, :, columns(t)].bitcast(F32),
                                     ALU.subtract).then_inc(s["o_hl"], 1)
            tiles(gpsimd, lambda t, now, old: None, rest)

        @block.vector
        def _(dve):
            dve.memset(eps[:], EPS).then_inc(s["o_eps"], 1)
            dve.wait_ge(s["o_wts"], 48)

            def pool(t, now, old):
                dve.wait_ge(s["o_y"], t + 1)
                after(dve, s["o_mm"], t)
                dve.tensor_tensor(mT[:, G4:KD, :], mix_b[:, :].rearrange("p (g t) -> p g t", g=G4),
                                  scale[:].unsqueeze(2).to_broadcast((P, G4, P)), ALU.mult).then_inc(s["o_yev"], 1)

            def rest(t, ahead):
                dve.wait_ge(s["o_mm"], t + 1)
                dve.wait_ge(s["o_x_in"], 16 * t + 16)
                after(dve, s["o_st"], 16 * t)
                after(dve, s["o_h2"], t)
                for n in range(2):
                    dve.tensor_tensor(x1[:, n * 512:(n + 1) * 512], out_b[n][:, :], x_t[:, n * 512:(n + 1) * 512],
                                      ALU.add).then_inc(s["o_x1"], 1)
                ahead()
                dve.wait_ge(s["o_std"], t + 1)
                dve.reciprocal(rstd[:], ss[:]).then_inc(s["o_rstd"], 1)
                dve.wait_ge(s["o_tr"], t + 1)
                after(dve, s["o_hl"], t)
                dve.wait_ge(s["o_late"], 32)
                for n in range(2):
                    dve.tensor_tensor(h2T[:, 4 * n:4 * n + 4, :],
                                      turn_b[n][:, :].rearrange("p (g t) -> p g t", g=4),
                                      g_ffn[:, 4 * n:4 * n + 4].unsqueeze(2).to_broadcast((P, 4, P)),
                                      ALU.mult).then_inc(s["o_h2T"], 1)
            tiles(dve, pool, rest)


def router(nc, a, h2, picks):
    h2h, h2l = h2
    with ExitStack() as ctx:
        def sb(name, shape, dt=F32):
            return ctx.enter_context(nc.sbuf_tensor(name, shape, dt))

        ident = sb("r_ident", [P, P])
        iota = sb("r_iota", [P, P])
        keysT = sb("r_keysT", [P, HP, NK])
        w = [sb(f"r_w{e}", [P, KD, P]) for e in range(2)]
        wh = [sb(f"r_wh{e}", [P, KD, P], F32R) for e in range(2)]
        wl = [sb(f"r_wl{e}", [P, KD, P], F32R) for e in range(2)]
        qT = [sb(f"r_qT{e}", [P, NPAD]) for e in range(2)]
        scores = [sb(f"r_scores{e}", [P, TILES, 2, NK]) for e in range(2)]
        val = sb("c_val", [P, TILES, 2, TOPK])
        idx = sb("c_idx", [P, TILES, 2, TOPK], U32)
        idf = sb("c_idf", [P, TILES, 2, TOPK])
        best = sb("c_best", [P, TILES, TOPK])
        at = sb("c_at", [P, TILES, TOPK], U32)
        ab = sb("c_ab", [P, 2, TILES * TOPK], U32)
        abf = sb("c_abf", [P, 2, TILES * TOPK])
        eq = [sb(f"c_eq{k}", [P, TILES * TOPK, TOPK]) for k in range(2)]
        gate = sb("c_gate", [P, TILES, TOPK])
        out = sb("c_out", [P, 3, TILES, H * TOPK])
        tot = sb("c_tot", [P, TILES])
        inv = sb("c_inv", [P, TILES])
        pad = sb("c_pad", [P, 2])
        bank = lambda n: ctx.enter_context(nc.psum_tensor(n, [P, 512], F32))
        q_b = [bank("r_q0"), bank("r_q1")]
        s_b = [bank(f"r_s{c}") for c in range(3)]
        turn = [bank(f"c_turn{c}") for c in range(3)]
        s = with_sems(nc, ctx, """r_in r_win0 r_win1 r_wh r_wl r_q r_qev r_s r_sev
            r_zero c_pad c_m1 c_i1 c_r c_m2 c_i2 c_idf c_cand c_fm1 c_fi1 c_fr c_fm2 c_fi2 c_ab c_abf c_eq c_pk
            c_sub c_exp c_tot c_inv c_gate c_tr c_ev""")
        PICK = 5
        w_in = [s["r_win0"], s["r_win1"]]
        block = ctx.enter_context(nc.Block())

        def heads(eng, first, tail):
            first(0, 0, None, False)
            with eng.Fori(0, H // 2 - 1) as i:
                first(2 * i + 1, 1, tail(2 * i, 0), False)
                first(2 * i + 2, 0, tail(2 * i + 1, 1), False)
            first(H - 1, 1, tail(H - 2, 0), True)
            tail(H - 1, 1)()

        @block.sync
        def _(sp):
            def weights(j, e):
                sp.dma_start(w[e][:], a["w_pq"][bass.ds(j, 1)].rearrange("o p k c -> (o p) k c")
                             ).then_inc(w_in[e], 16)
            weights(0, 0)
            weights(1, 1)
            for dst, src in ((keysT, "keysT"), (ident, "ident"), (iota, "iota")):
                sp.dma_start(dst[:], a[src]).then_inc(s["r_in"], 16)
            with sp.Fori(0, HP // 2 - 1) as m:
                for e in range(2):
                    j = 2 * m + e + 2
                    sp.wait_ge(s["r_wl"], 2 * m + e + 1)
                    weights(j, e)

        @block.tensor
        def _(pe):
            pe.wait_ge(s["r_zero"], 2)

            def queries(j, e, b):
                pe.wait_ge(s["r_wl"], j + 1)
                after(pe, s["r_qev"], 3 * j + b - 1)
                cols = slice(b * TB, (b + 1) * TB)
                o = q_b[(e + b) % 2][:, 0:TB]
                for k in range(KD):
                    pe.matmul(o, wh[e][:, k, :], h2h[:, k, cols], start=k == 0, stop=False)
                    pe.matmul(o, wh[e][:, k, :], h2l[:, k, cols], start=False, stop=False)
                    mm = pe.matmul(o, wl[e][:, k, :], h2h[:, k, cols], start=False, stop=k == KD - 1)
                mm.then_inc(s["r_q"], 1)

            def score(j, e):
                pe.wait_ge(s["r_qev"], 3 * j + 3)
                after(pe, s["r_sev"], 3 * j)
                for t in range(TILES):
                    mm = pe.matmul(s_b[t // 4][:, (t % 4) * NK:(t % 4 + 1) * NK], qT[e][:, t * P:(t + 1) * P],
                                   keysT[:, bass.ds(j, 1), :], start=True, stop=True)
                mm.then_inc(s["r_s"], 1)

            def first(m, e, late, last):
                queries(2 * m, 0, 0)
                queries(2 * m, 0, 1)
                queries(2 * m, 0, 2)
                queries(2 * m + 1, 1, 0)
                if isinstance(m, int) and m == 0:
                    pe.wait_ge(s["r_in"], 48)
                score(2 * m, 0)
                queries(2 * m + 1, 1, 1)
                queries(2 * m + 1, 1, 2)
                score(2 * m + 1, 1)
            heads(pe, first, lambda m, e: lambda: None)
            for t in range(TILES):
                if t == 0:
                    pe.wait_ge(s["c_gate"], H)
                    pe.wait_ge(s["c_pk"], 2 * PICK * H)
                after(pe, s["c_ev"], t - 2)
                for k in range(3):
                    mm = pe.transpose(turn[t % 3][:, k * P:(k + 1) * P], out[:, k, t, :], ident[:])
                mm.then_inc(s["c_tr"], 1)

        @block.scalar
        def _(act):
            def split(j, e, n):
                act.wait_ge(w_in[e], 16 * n)
                act.activation(wh[e][:], w[e][:], ACT.Copy).then_inc(s["r_wh"], 1)
            split(0, 0, 1)

            def query(j, e, b):
                act.wait_ge(s["r_q"], 3 * j + b + 1)
                after(act, s["r_s"], j - 1)
                act.activation(qT[e][:, b * TB:(b + 1) * TB], q_b[(e + b) % 2][:, 0:TB],
                               ACT.Copy).then_inc(s["r_qev"], 1)

            def score(m, e, half):
                act.wait_ge(s["r_s"], 2 * m + half + 1)
                after(act, s["c_fi2"], m - 1)
                for c in range(3):
                    n = min(4, TILES - 4 * c)
                    act.activation(scores[e][:, 4 * c:4 * c + n, half, :],
                                   s_b[c][:, 0:n * NK].rearrange("p (t n) -> p t n", t=n),
                                   ACT.Copy).then_inc(s["r_sev"], 1)

            def first(m, e, late, last):
                query(2 * m, 0, 0)
                split(2 * m + 1, 1, m + 1)
                query(2 * m, 0, 1)
                query(2 * m, 0, 2)
                query(2 * m + 1, 1, 0)
                if not last:
                    split(2 * m + 2, 0, m + 2)
                score(m, e, 0)
                query(2 * m + 1, 1, 1)
                query(2 * m + 1, 1, 2)
                if late:
                    late()
                score(m, e, 1)

            def tail(m, e):
                def exp():
                    act.wait_ge(s["c_sub"], m + 1)
                    act.activation(gate[:], gate[:], ACT.Exp).then_inc(s["c_exp"], 1)
                return exp
            heads(act, first, tail)
            for t in range(TILES):
                act.wait_ge(s["c_tr"], t + 1)
                act.activation(picks[:, :, t * P:(t + 1) * P], turn[t % 3][:, 0:3 * P].rearrange("p (k t) -> p k t", k=3),
                               ACT.Copy).then_inc(s["c_ev"], 1)

        @block.gpsimd
        def _(pool):
            def split(j, e):
                pool.wait_ge(s["r_wh"], j + 1)
                after(pool, s["r_q"], 3 * (j - 1))
                pool.tensor_tensor(wl[e][:], w[e][:], wh[e][:].bitcast(F32), ALU.subtract).then_inc(s["r_wl"], 1)
            split(0, 0)

            def first(m, e, late, last):
                split(2 * m + 1, 1)
                if not last:
                    split(2 * m + 2, 0)
                if late:
                    late()

            def tail(m, e):
                def pick():
                    for k in range(2):
                        pool.wait_ge(s["c_eq"], 2 * m + k + 1)
                        e4 = eq[k][:].rearrange("p (t k) i -> p t k i", t=TILES)
                        pool.tensor_tensor(e4, e4, idf[:, :, k, :].unsqueeze(2).to_broadcast((P, TILES, TOPK, TOPK)),
                                           ALU.mult).then_inc(s["c_pk"], 1)
                        for step, n in enumerate((8, 4, 2, 1)):
                            pool.wait_ge(s["c_pk"], PICK * (2 * m + k) + step + 1)
                            o = e4[:, :, :, 0:n] if n > 1 else out[:, 1 + k, :, bass.ds(m * TOPK, TOPK)].unsqueeze(3)
                            pool.tensor_tensor(o, e4[:, :, :, 0:n], e4[:, :, :, n:2 * n],
                                               ALU.add).then_inc(s["c_pk"], 1)
                return pick
            heads(pool, first, tail)

        @block.vector
        def _(dve):
            dve.memset(pad[:], 0.0).then_inc(s["c_pad"], 1)
            for e in range(2):
                dve.memset(qT[e][:, NT:NPAD], 0.0).then_inc(s["r_zero"], 1)
            dve.wait_ge(s["c_pad"], 1)
            dve.wait_ge(s["r_in"], 48)

            def settled(name, value):
                dve.wait_ge(s[name], value)
                dve.tensor_copy(pad[:, 1:2], pad[:, 0:1])

            def top16(src, n, v, i, m, sems):
                m1, i1, r, m2, i2 = sems
                for q in range(n):
                    op = dve.max(v[:, q, 0:8], src[:, q, :])
                op.then_inc(s[m1], 1)
                settled(m1, m + 1)
                for q in range(n):
                    op = dve.max_index(i[:, q, 0:8], v[:, q, 0:8], src[:, q, :])
                op.then_inc(s[i1], 1)
                settled(i1, m + 1)
                for q in range(n):
                    op = dve.match_replace(out=src[:, q, :], in_to_replace=v[:, q, 0:8], in_values=src[:, q, :],
                                           imm_value=NEG)
                op.then_inc(s[r], 1)
                settled(r, m + 1)
                for q in range(n):
                    op = dve.max(v[:, q, 8:16], src[:, q, :])
                op.then_inc(s[m2], 1)
                settled(m2, m + 1)
                for q in range(n):
                    op = dve.max_index(i[:, q, 8:16], v[:, q, 8:16], src[:, q, :])
                op.then_inc(s[i2], 1)

            def first(m, e, late, last):
                cols = bass.ds(m * TOPK, TOPK)
                st = scores[e][:].rearrange("p t k n -> p (t k) n")
                cand = scores[e][:].rearrange("p t k n -> p t (k n)")
                settled("r_sev", 6 * m + 6)
                top16(st, 2 * TILES, val[:].rearrange("p t k i -> p (t k) i"), idx[:].rearrange("p t k i -> p (t k) i"),
                      m, ("c_m1", "c_i1", "c_r", "c_m2", "c_i2"))
                dve.wait_ge(s["c_i2"], m + 1)
                after(dve, s["c_pk"], 2 * PICK * m)
                dve.tensor_copy(idf[:], idx[:]).then_inc(s["c_idf"], 1)
                dve.tensor_tensor(cand.rearrange("p t (i j) -> p t i j", j=TOPK),
                                  val[:, :, 0, :].unsqueeze(3).to_broadcast((P, TILES, TOPK, TOPK)),
                                  val[:, :, 1, :].unsqueeze(2).to_broadcast((P, TILES, TOPK, TOPK)),
                                  ALU.add).then_inc(s["c_cand"], 1)
                settled("c_cand", m + 1)
                top16(cand, TILES, best, at, m, ("c_fm1", "c_fi1", "c_fr", "c_fm2", "c_fi2"))
                after(dve, s["c_gate"], m)
                dve.tensor_tensor(gate[:], best[:], best[:, :, 0:1].to_broadcast((P, TILES, TOPK)),
                                  ALU.subtract).then_inc(s["c_sub"], 1)
                dve.wait_ge(s["c_fi2"], m + 1)
                flat = at[:].rearrange("p t k -> p (t k)")
                dve.tensor_scalar(ab[:, 0, :], flat, 4, None, ALU.logical_shift_right).then_inc(s["c_ab"], 1)
                dve.tensor_scalar(ab[:, 1, :], flat, 15, None, ALU.bitwise_and).then_inc(s["c_ab"], 1)
                dve.wait_ge(s["c_ab"], 2 * m + 2)
                dve.tensor_copy(abf[:], ab[:]).then_inc(s["c_abf"], 1)
                dve.wait_ge(s["c_abf"], m + 1)
                dve.wait_ge(s["c_idf"], m + 1)
                for k in range(2):
                    dve.tensor_tensor(eq[k][:], abf[:, k, :].unsqueeze(2).to_broadcast((P, TILES * TOPK, TOPK)),
                                      iota[:, 0:TOPK].unsqueeze(1).to_broadcast((P, TILES * TOPK, TOPK)),
                                      ALU.is_equal).then_inc(s["c_eq"], 1)
                dve.wait_ge(s["c_exp"], m + 1)
                dve.tensor_reduce(tot[:], gate[:], AX, ALU.add).then_inc(s["c_tot"], 1)
                dve.wait_ge(s["c_tot"], m + 1)
                dve.reciprocal(inv[:], tot[:]).then_inc(s["c_inv"], 1)
                dve.wait_ge(s["c_inv"], m + 1)
                dve.tensor_tensor(out[:, 0, :, cols], gate[:], inv[:].unsqueeze(2).to_broadcast((P, TILES, TOPK)),
                                  ALU.mult).then_inc(s["c_gate"], 1)
            heads(dve, first, lambda m, e: lambda: None)


def gate_matrix(nc, a, picks):
    GRP = 4
    NG = GT // GRP
    RING = 4
    BODY = 2 * NG
    assert BODY % RING == 0
    on_act = [q for q in range(BODY) if q % 3 == 2]
    on_pool = [q for q in range(BODY) if q % 3 != 2]
    with ExitStack() as ctx:
        def sb(name, shape, dt=F32):
            return ctx.enter_context(nc.sbuf_tensor(name, shape, dt))

        iota = sb("g_iota", [P, P])
        hot = [sb(f"g_hot{r}", [P, 2, GRP, NK]) for r in range(RING)]
        stage = [sb(f"g_stage{e}", [P, NK, GT]) for e in range(2)]
        acc = [ctx.enter_context(nc.psum_tensor(f"g_acc{r}", [P, 512], F32)) for r in range(RING)]
        s = with_sems(nc, ctx, "g_in g_hot g_act g_pool g_mm g_ev g_st0 g_st1")
        stored = [s["g_st0"], s["g_st1"]]
        block = ctx.enter_context(nc.Block())

        @block.sync
        def _(sp):
            sp.dma_start(iota[:], a["iota"]).then_inc(s["g_in"], 16)
            with sp.Fori(0, GB // 2) as m:
                for e in range(2):
                    sp.wait_ge(s["g_ev"], (2 * m + e + 1) * NG)
                    sp.dma_start(a["gates_d"][:, bass.ds(2 * m + e, 1)].rearrange("p o i t -> p (o i t)"),
                                 stage[e][:].rearrange("p i t -> p (i t)")).then_inc(stored[e], 16)
            for e in range(2):
                sp.wait_ge(stored[e], 16 * (GB // 2))

        @block.vector
        def _(dve):
            dve.wait_ge(s["g_in"], 16)
            with dve.Fori(0, GB // 2) as m:
                for q in range(BODY):
                    dve.wait_ge(s["g_mm"], BODY * m + max(q - RING + 1, 0))
                    dve.tensor_tensor(hot[q % RING][:],
                                      iota[:].unsqueeze(1).unsqueeze(1).to_broadcast((P, 2, GRP, NK)),
                                      picks[:, 1:3, bass.ds(2 * GT * m + GRP * q, GRP)].unsqueeze(3)
                                      .to_broadcast((P, 2, GRP, NK)), ALU.is_equal).then_inc(s["g_hot"], 1)

        @block.gpsimd
        def _(pool):
            with pool.Fori(0, GB // 2) as m:
                for q in on_pool:
                    two = hot[q % RING][:, 1]
                    pool.wait_ge(s["g_hot"], BODY * m + q + 1)
                    pool.tensor_tensor(two, two, picks[:, 0, bass.ds(2 * GT * m + GRP * q, GRP)].unsqueeze(2)
                                       .to_broadcast((P, GRP, NK)), ALU.mult).then_inc(s["g_pool"], 1)

        @block.tensor
        def _(pe):
            with pe.Fori(0, GB // 2) as m:
                for q in range(BODY):
                    if q in on_act:
                        pe.wait_ge(s["g_act"], len(on_act) * m + on_act.index(q) + 1)
                    else:
                        pe.wait_ge(s["g_pool"], len(on_pool) * m + on_pool.index(q) + 1)
                    pe.wait_ge(s["g_hot"], BODY * m + q + 1)
                    pe.wait_ge(s["g_ev"], BODY * m + max(q - RING + 1, 0))
                    for j in range(GRP):
                        mm = pe.matmul(acc[q % RING][:, j * NK:(j + 1) * NK], hot[q % RING][:, 0, j, :],
                                       hot[q % RING][:, 1, j, :], start=True, stop=True)
                    mm.then_inc(s["g_mm"], 1)

        @block.scalar
        def _(act):
            LAG = 2
            with act.Fori(0, GB // 2) as m:
                for q in range(BODY + LAG):
                    if q in on_act:
                        act.wait_ge(s["g_hot"], BODY * m + q + 1)
                        for j in range(GRP):
                            row = hot[q % RING][:, 1, j, :]
                            op = act.activation(row, row, ACT.Copy,
                                                scale=picks[:, 0, bass.ds(2 * GT * m + GRP * q + j, 1)])
                        op.then_inc(s["g_act"], 1)
                    if q < LAG:
                        continue
                    e, g = divmod(q - LAG, NG)
                    if g == 0:
                        act.wait_ge(stored[e], 16 * m)
                    act.wait_ge(s["g_mm"], BODY * m + q - LAG + 1)
                    act.activation(stage[e][:, :, GRP * g:GRP * (g + 1)],
                                   acc[(q - LAG) % RING][:, :].rearrange("p (t i) -> p i t", t=GRP),
                                   ACT.Copy).then_inc(s["g_ev"], 1)


def experts(nc, a, h2, y):
    h2h, h2l = h2
    LAST = NK - 1
    with ExitStack() as ctx:
        def sb(name, shape, dt=F32):
            return ctx.enter_context(nc.sbuf_tensor(name, shape, dt))

        u = [sb(f"e_u{r}", [P, KD, P]) for r in range(2)]
        uh = [sb(f"e_uh{r}", [P, KD, P], F32R) for r in range(2)]
        ul = [sb(f"e_ul{r}", [P, KD, P], F32R) for r in range(2)]
        v = sb("e_v", [P, 2, D])
        vh = sb("e_vh", [P, 2, D], F32R)
        vl = sb("e_vl", [P, 2, D], F32R)
        gate = [sb(f"e_gate{r}", [P, GB, 2, GT]) for r in range(2)]
        gelu = [sb(f"e_gelu{r}", [P, TB]) for r in range(2)]
        wf = [sb(f"e_wf{r}", [P, TB]) for r in range(2)]
        wh = [sb(f"e_wh{r}", [P, NT], F32R) for r in range(4)]
        wl = [sb(f"e_wl{r}", [P, NT], F32R) for r in range(4)]
        a_b = [ctx.enter_context(nc.psum_tensor(f"e_a{r}", [P, 512], F32)) for r in range(2)]
        y_b = [ctx.enter_context(nc.psum_tensor(f"e_y{r}", [P, 512], F32)) for r in range(4)]
        s = with_sems(nc, ctx, """e_uin0 e_uin1 e_vin e_gin0 e_gin1 e_uh e_ul e_vh e_vl e_a e_gelu e_wf e_wh e_wl
            e_y e_yadd""")
        u_in = [s["e_uin0"], s["e_uin1"]]
        g_in = [s["e_gin0"], s["e_gin1"]]
        block = ctx.enter_context(nc.Block())
        YB = 3 * KD
        GB3 = GB // 3

        @block.sync
        def _(sp):
            def load_u(j, r):
                after(sp, s["e_ul"], j - 1)
                sp.dma_start(u[r][:], a["uT"][bass.ds(j, 1)].rearrange("o p k c -> (o p) k c")).then_inc(u_in[r], 16)

            def load_v(p):
                after(sp, s["e_vl"], p)
                sp.dma_start(v[:], a["v"][:, bass.ds(2 * p, 2), :]).then_inc(s["e_vin"], 16)

            def load_gate(p, r):
                after(sp, s["e_wf"], 6 * (p - 1))
                sp.dma_start(gate[r][:], a["gates_d"][:, :, bass.ds(2 * p, 2), :]).then_inc(g_in[r], 16)

            load_u(0, 0)
            load_gate(0, 0)
            load_u(1, 1)
            load_v(0)

            def body(i, last):
                load_u(4 * i + 2, 0)
                load_gate(2 * i + 1, 1)
                load_u(4 * i + 3, 1)
                load_v(2 * i + 1)
                if not last:
                    load_u(4 * i + 4, 0)
                    load_gate(2 * i + 2, 0)
                    load_u(4 * i + 5, 1)
                    load_v(2 * i + 2)
            body(0, False)
            with sp.Fori(1, NK // 4 - 1) as i:
                body(i, False)
            body(NK // 4 - 1, True)

        @block.tensor
        def _(pe):
            def make_a(j, q, r):
                pe.wait_ge(s["e_uh"], j + 1)
                pe.wait_ge(s["e_ul"], j + 1)
                for b in range(3):
                    after(pe, s["e_gelu"], 3 * j + b - 1)
                    o = a_b[(r + b) % 2][:, 0:TB]
                    cols = slice(b * TB, (b + 1) * TB)
                    for k in range(KD):
                        pe.matmul(o, uh[q][:, k, :], h2h[:, k, cols], start=k == 0, stop=False)
                        pe.matmul(o, uh[q][:, k, :], h2l[:, k, cols], start=False, stop=False)
                        mm = pe.matmul(o, ul[q][:, k, :], h2h[:, k, cols], start=False, stop=k == KD - 1)
                    mm.then_inc(s["e_a"], 1)

            def add_values(p, slots):
                pe.wait_ge(s["e_vh"], p + 1)
                pe.wait_ge(s["e_vl"], p + 1)
                pe.wait_ge(s["e_wl"], 6 * p + 6)
                n = 0
                for k in range(KD):
                    for b in range(3):
                        after(pe, s["e_yadd"], YB * p + max(n - 3, 0))
                        cols = slice(b * TB, (b + 1) * TB)
                        o = y_b[n % 4][:, 0:TB]
                        for c, r in enumerate(slots):
                            h, l = vh[:, c, k * P:(k + 1) * P], vl[:, c, k * P:(k + 1) * P]
                            pe.matmul(o, h, wh[r][:, cols], start=c == 0, stop=False)
                            pe.matmul(o, h, wl[r][:, cols], start=False, stop=False)
                            mm = pe.matmul(o, l, wh[r][:, cols], start=False, stop=c == 1)
                        mm.then_inc(s["e_y"], 1)
                        n += 1

            def body(i, last):
                make_a(4 * i + 1, 1, 1)
                make_a(4 * i + 2, 0, 0)
                add_values(2 * i, (0, 1))
                make_a(4 * i + 3, 1, 1)
                if not last:
                    make_a(4 * i + 4, 0, 0)
                add_values(2 * i + 1, (2, 3))
            make_a(0, 0, 0)
            with pe.Fori(0, NK // 4 - 1) as i:
                body(i, False)
            body(NK // 4 - 1, True)

        @block.scalar
        def _(act):
            def split_u(j, r):
                act.wait_ge(u_in[r], 16 * (j // 2 + 1) if isinstance(j, int) else 8 * (j - r) + 16)
                after(act, s["e_a"], 3 * (j - 1))
                act.activation(uh[r][:], u[r][:], ACT.Copy).then_inc(s["e_uh"], 1)

            def split_v(p):
                act.wait_ge(s["e_vin"], 16 * p + 16)
                after(act, s["e_y"], YB * p)
                act.activation(vh[:], v[:], ACT.Copy).then_inc(s["e_vh"], 1)

            def weigh(j, r, slot):
                for b in range(3):
                    act.wait_ge(s["e_a"], 3 * j + b + 1)
                    after(act, s["e_wf"], 3 * j + b - 1)
                    act.activation(gelu[(r + b) % 2][:], a_b[(r + b) % 2][:, 0:TB], ACT.Gelu).then_inc(s["e_gelu"], 1)
                    act.wait_ge(s["e_wf"], 3 * j + b + 1)
                    act.activation(wh[slot][:, b * TB:(b + 1) * TB], wf[(r + b) % 2][:], ACT.Copy
                                   ).then_inc(s["e_wh"], 1)

            def body(i, last):
                split_u(4 * i + 2, 0)
                weigh(4 * i + 1, 1, 1)
                split_v(2 * i)
                split_u(4 * i + 3, 1)
                weigh(4 * i + 2, 0, 2)
                if not last:
                    split_u(4 * i + 4, 0)
                weigh(4 * i + 3, 1, 3)
                split_v(2 * i + 1)
                if not last:
                    split_u(4 * i + 5, 1)
                    weigh(4 * i + 4, 0, 0)
            split_u(0, 0)
            split_u(1, 1)
            weigh(0, 0, 0)
            body(0, False)
            with act.Fori(1, NK // 4 - 1) as i:
                body(i, False)
            body(NK // 4 - 1, True)

        @block.vector
        def _(dve):
            def split_u(j, r):
                after(dve, s["e_a"], 3 * (j - 1))
                dve.wait_ge(s["e_uh"], j + 1)
                dve.tensor_tensor(ul[r][:], u[r][:], uh[r][:].bitcast(F32), ALU.subtract).then_inc(s["e_ul"], 1)

            def split_v(p):
                after(dve, s["e_y"], YB * p)
                dve.wait_ge(s["e_vh"], p + 1)
                dve.tensor_tensor(vl[:], v[:], vh[:].bitcast(F32), ALU.subtract).then_inc(s["e_vl"], 1)

            def weigh(j, r, slot, g, gcount, free):
                dve.wait_ge(g_in[g], gcount)
                after(dve, s["e_y"], free)
                for b in range(3):
                    dve.wait_ge(s["e_gelu"], 3 * j + b + 1)
                    after(dve, s["e_wh"], 3 * j + b - 1)
                    w3 = lambda x: x.rearrange("p (b t) -> p b t", t=GT)
                    dve.tensor_tensor(w3(wf[(r + b) % 2][:]), w3(gelu[(r + b) % 2][:]),
                                      gate[g][:, GB3 * b:GB3 * (b + 1), slot % 2, :], ALU.mult).then_inc(s["e_wf"], 1)
                    dve.wait_ge(s["e_wh"], 3 * j + b + 1)
                    cols = slice(b * TB, (b + 1) * TB)
                    dve.tensor_tensor(wl[slot][:, cols], wf[(r + b) % 2][:], wh[slot][:, cols].bitcast(F32),
                                      ALU.subtract).then_inc(s["e_wl"], 1)

            def add(p, first):
                n = 0
                for k in range(KD):
                    for b in range(3):
                        dve.wait_ge(s["e_y"], YB * p + n + 1)
                        after(dve, s["e_yadd"], YB * p)
                        cols = slice(b * TB, (b + 1) * TB)
                        if first:
                            dve.tensor_copy(y[:, k, cols], y_b[n % 4][:, 0:TB]).then_inc(s["e_yadd"], 1)
                        else:
                            dve.tensor_tensor(y[:, k, cols], y_b[n % 4][:, 0:TB], y[:, k, cols],
                                              ALU.add).then_inc(s["e_yadd"], 1)
                        n += 1

            def body(i, first, last):
                split_u(4 * i + 2, 0)
                weigh(4 * i + 1, 1, 1, 0, 16 * i + 16, YB * 2 * i)
                split_v(2 * i)
                split_u(4 * i + 3, 1)
                weigh(4 * i + 2, 0, 2, 1, 16 * i + 16, YB * 2 * i)
                if not last:
                    split_u(4 * i + 4, 0)
                add(2 * i, first)
                weigh(4 * i + 3, 1, 3, 1, 16 * i + 16, YB * 2 * i)
                split_v(2 * i + 1)
                if not last:
                    split_u(4 * i + 5, 1)
                    weigh(4 * i + 4, 0, 0, 0, 16 * i + 32, YB * (2 * i + 1))
                add(2 * i + 1, False)
            split_u(0, 0)
            split_u(1, 1)
            weigh(0, 0, 0, 0, 16, 0)
            body(0, True, False)
            with dve.Fori(1, NK // 4 - 1) as i:
                body(i, False, False)
            body(NK // 4 - 1, False, True)


def finish(nc, a, y):
    with ExitStack() as ctx:
        ident = ctx.enter_context(nc.sbuf_tensor("z_ident", [P, P], F32))
        x1 = ctx.enter_context(nc.sbuf_tensor("z_x1", [P, TILES, D], F32))
        bank = [ctx.enter_context(nc.psum_tensor(f"z_b{e}", [P, D], F32)) for e in range(2)]
        s = with_sems(nc, ctx, "z_id z_in0 z_in1 z_in2 z_tr z_add z_st")
        x_in = [s["z_in0"], s["z_in1"], s["z_in2"]]
        rows = [P] * PT_TILES + [NS]
        block = ctx.enter_context(nc.Block())

        @block.sync
        def _(sp):
            sp.dma_start(ident[:], a["ident"]).then_inc(s["z_id"], 16)
            for t, n in enumerate(rows):
                sp.dma_start(x1[0:n, t, :], a["x1_d"][t * P:t * P + n, :]).then_inc(x_in[t // 3], 16)
            for t, n in enumerate(rows):
                sp.wait_ge(s["z_add"], 2 * t + 2)
                sp.dma_start(a["y_all"][t * P:t * P + n, :], x1[0:n, t, :]).then_inc(s["z_st"], 16)
            sp.wait_ge(s["z_st"], 16 * TILES)

        @block.tensor
        def _(pe):
            pe.wait_ge(s["z_id"], 16)
            for t, n in enumerate(rows):
                if t >= 2:
                    pe.wait_ge(s["z_add"], 2 * (t - 1))
                for k in range(KD):
                    mm = pe.transpose(bank[t % 2][0:n, k * P:(k + 1) * P], y[:, k, t * P:t * P + n], ident[:])
                mm.then_inc(s["z_tr"], 1)

        @block.vector
        def _(dve):
            for t, n in enumerate(rows):
                dve.wait_ge(s["z_tr"], t + 1)
                dve.wait_ge(x_in[t // 3], 16 * 3)
                for c in range(2):
                    cols = slice(c * 512, (c + 1) * 512)
                    dve.tensor_tensor(x1[0:n, t, cols], bank[t % 2][0:n, cols], x1[0:n, t, cols],
                                      ALU.add).then_inc(s["z_add"], 1)


def build_step(nc, a):
    a["pin_d"] = nc.dram_tensor("pin_d", [NPAD, PW], F32).ap()
    a["mixT_d"] = nc.dram_tensor("mixT_d", [P, G4, NPAD], F32).ap()
    a["x1_d"] = nc.dram_tensor("x1_d", [NPAD, D], F32).ap()
    a["gates_d"] = nc.dram_tensor("gates_d", [P, GB, NK, GT], F32).ap()
    with ExitStack() as attention:
        def sb(name, shape, dt=F32):
            return attention.enter_context(nc.sbuf_tensor(name, shape, dt))
        qkT = sb("qkT", [P, 2 * H, NPAD])
        kept = {"ident": sb("ident_kept", [P, P]), "w_uk": sb("w_uk_kept", [P, CT, H * NOPE]),
                "w_uv": sb("w_uv_kept", [P, CT, H * VD]), "w_ukT": sb("w_ukT_kept", [NOPE, H, KVL]),
                "g_k": sb("g_k_kept", [HD, 1]), "newmask": sb("newmask_kept", [DEC_S, H, DEC_S]),
                "table": sb("table_kept", [1, DEC_B * PAGES], I32)}
        with nc.sbuf_tensor("vall", [P, TILES, H * VD], F32) as vall:
            mixer_front(nc, a, qkT, vall, kept)
            prompt_attention(nc, a, qkT, vall)
        sample_attention(nc, a, qkT, kept)
    with nc.sbuf_tensor("h2h", [P, KD, NT], F32R) as h2h, nc.sbuf_tensor("h2l", [P, KD, NT], F32R) as h2l:
        mixer_out(nc, a, (h2h, h2l))
        with nc.sbuf_tensor("picks", [P, 3, NPAD], F32) as picks:
            router(nc, a, (h2h, h2l), picks)
            gate_matrix(nc, a, picks)
        with nc.sbuf_tensor("y", [P, KD, NT], F32) as y:
            experts(nc, a, (h2h, h2l), y)
            finish(nc, a, y)




def shape_constants():
    f = np.float32
    pos = np.zeros(NPAD, f)
    pos[:SEQ] = np.arange(SEQ)
    pos[SEQ:NT] = PAST + np.tile(np.arange(DEC_S), DEC_B)
    inv = (np.float32(10000.0) ** (-np.arange(HALF, dtype=f) / f(HALF))).astype(f)
    ang = (pos[:, None] * inv[None, :]).astype(f)
    cos, sin = np.cos(ang), np.sin(ang)
    tiles = lambda m: np.ascontiguousarray(m.reshape(TILES, P, ROPE).transpose(1, 0, 2).astype(f))
    out = {
        "ident": np.eye(P, dtype=f),
        "rope_c": tiles(np.concatenate([cos, cos], 1)),
        "rope_s": tiles(np.concatenate([-sin, sin], 1)),
        "causal": np.where(np.arange(P)[None, :] <= np.arange(P)[:, None], f(0), f(NEG)),
        "iota": np.tile(np.arange(P, dtype=f), (P, 1)),
    }
    band = np.zeros((P, 5, G4, P), f)
    t = np.arange(P)
    for g, w in enumerate(WINDOWS):
        for kind, at, count in ((0, 0, np.minimum(w, t + 1)), (1, 0, np.full(P, w)), (2, -P, np.full(P, w))):
            src = t[:, None] + at
            inside = (src <= t[None, :]) & (src > t[None, :] - w)
            band[:, kind, g, :] = np.where(inside, f(1) / count[None, :].astype(f), f(0)) - (src == t[None, :])
        for b in range(DEC_B):
            for o in range(DEC_S):
                for r in range(DEC_S):
                    band[b * DEC_S + r, 3, g, b * DEC_S + o] = (r <= o and r > o - w) / f(w) - (r == o)
                for r in range(PSTATE):
                    band[b * PSTATE + r, 4, g, b * DEC_S + o] = (r - PSTATE > o - w) / f(w)
    out["band"] = band
    ok = np.arange(DEC_S)[:, None] <= np.arange(DEC_S)[None, :]
    out["newmask"] = np.ascontiguousarray(np.broadcast_to(np.where(ok, f(0), f(NEG))[:, None, :], (DEC_S, H, DEC_S)))
    return out


def layouts(i):
    f = np.float32
    c = np.ascontiguousarray
    x = np.zeros((NPAD, D), f)
    x[:SEQ], x[SEQ:NT] = i["x_prompt"][0], i["x_sample"].reshape(NS, D)
    rows = lambda w, k: c(w.reshape(k, P, -1).transpose(1, 0, 2))
    lat, kr = i["cache_kv_latent"], i["cache_k_rope"]
    n_phys = lat.shape[0]
    page = np.zeros((n_phys, P, KVL + ROPE), f)
    page[:, :, 0:KVL] = lat.transpose(0, 2, 1).reshape(n_phys, CT, P, P).transpose(0, 2, 1, 3).reshape(n_phys, P, KVL)
    page[:, :, KVL:] = kr
    state = np.zeros((P, PW), f)
    state[:DEC_B * PSTATE] = i["state_pool"].reshape(DEC_B * PSTATE, PW)
    u = i["peer_u"].reshape(NK, NK, KD, P)
    v = i["peer_v"].reshape(NK, NK, D)
    return {
        "x": x,
        "xT": c(x.T.reshape(KD, P, NPAD).transpose(1, 0, 2)),
        "w_in": rows(i["w_in"], KD), "w_q_up": rows(i["w_q_up"], QT),
        "w_uk": rows(i["w_uk"].reshape(KVL, -1), CT), "w_uv": rows(i["w_uv"].reshape(KVL, -1), CT),
        "w_ukT": c(i["w_uk"].transpose(2, 1, 0)),
        "g_attn": c(i["g_attn"].reshape(KD, P).T), "g_q_lat": c(i["g_q_lat"].reshape(QT, P).T),
        "g_kv_lat": i["g_kv_lat"][None], "g_q_nope": i["g_q_nope"][None], "g_q_rope": i["g_q_rope"][None],
        "g_k_nope": i["g_k_nope"][None], "g_k_rope": i["g_k_rope"][None],
        "g_k_col": c(np.concatenate([i["g_k_nope"], i["g_k_rope"], i["g_k_rope"]])[:, None]),
        "page": page, "page_rows": lat, "page_krT": c(kr.transpose(0, 2, 1)),
        "page_table": i["page_table"].astype(np.int32, copy=False),
        "state": state, "state_pool": i["state_pool"],
        "w_pool": c(i["w_pool"].transpose(1, 0, 2)), "pool_scale": c(i["pool_scale"].reshape(G4, P).T),
        "w_o": rows(i["w_o"], KD), "g_ffn": c(i["g_ffn"].reshape(KD, P).T),
        "w_pq": c(i["w_pq"].reshape(KD, P, HP, P).transpose(2, 1, 0, 3)),
        "keysT": c(i["peer_keys"].reshape(HP, NK, P).transpose(2, 0, 1)),
        "uT": c(u.transpose(1, 3, 2, 0)),
        "v": v,
    }


OUTS = {
    "y_all": [NT, D], "kv_all": [NPAD, KVL], "kr_all": [NPAD, ROPE],
    "pool_prompt": [PSTATE, PW], "pool_sample": [DEC_B, PSTATE, PW],
}


def kernel(**inputs):
    import concourse.bacc as bacc
    from concourse.bass_utils import run_bass_kernel_spmd

    arrays = {**layouts({k: np.asarray(v) for k, v in inputs.items()}), **shape_constants()}
    nc = bacc.Bacc("TRN2", target_bir_lowering=False, num_devices=1)
    a = {n: nc.dram_tensor(n, list(v.shape), mybir.dt.from_np(v.dtype), kind="ExternalInput").ap()
         for n, v in arrays.items()}
    for n, shape in OUTS.items():
        a[n] = nc.dram_tensor(n, shape, F32, kind="ExternalOutput").ap()
    build_step(nc, a)
    r = run_bass_kernel_spmd(nc, [arrays], core_ids=[0]).results[0]
    return (r["y_all"][None, :SEQ], r["y_all"][SEQ:].reshape(DEC_B, DEC_S, D),
            r["kv_all"][None, :SEQ], r["kr_all"][None, :SEQ], r["pool_prompt"][None],
            r["kv_all"][SEQ:NT].reshape(DEC_B, DEC_S, KVL), r["kr_all"][SEQ:NT].reshape(DEC_B, DEC_S, ROPE),
            r["pool_sample"])
```
